# Optimizing a Trainium2 kernel written in Bass

```python
import jax, jax.numpy as jnp
from jax import lax
import numpy as np
import math

D_MODEL = 1024
BATCH = 1
SEQ = 512
DEPTH = 1

CHUNK = 64
GMLP_BLOCK = 128
GMLP_WIDTH = D_MODEL
GMLP_GROUPS = 8
GMLP_GROUP_DIM = GMLP_WIDTH // GMLP_GROUPS
MLSTM_HEADS = 4
MLSTM_HEAD_DIM = 256
MLSTM_WIDTH = MLSTM_HEADS * MLSTM_HEAD_DIM
CONV_K = 4
FFN_DIM = 4 * D_MODEL
EPS = 1e-6

OFF_U = 0
OFF_V = OFF_U + GMLP_WIDTH
OFF_Q = OFF_V + GMLP_WIDTH
OFF_K = OFF_Q + MLSTM_WIDTH
OFF_MV = OFF_K + MLSTM_WIDTH
OFF_O = OFF_MV + MLSTM_WIDTH
OFF_I = OFF_O + MLSTM_WIDTH
OFF_F = OFF_I + MLSTM_HEADS
OFF_GA = OFF_F + MLSTM_HEADS
OFF_GB = OFF_GA + D_MODEL
IN_COLS = OFF_GB + D_MODEL


def rmsnorm(x, g):
    xf = x.astype(jnp.float32)
    y = xf * lax.rsqrt(jnp.mean(xf * xf, axis=-1, keepdims=True) + EPS)
    return y.astype(x.dtype) * g

def layernorm(x, g, b):
    xf = x.astype(jnp.float32)
    mu = jnp.mean(xf, axis=-1, keepdims=True)
    var = jnp.mean(jnp.square(xf - mu), axis=-1, keepdims=True)
    y = (xf - mu) * lax.rsqrt(var + EPS)
    return y.astype(x.dtype) * g + b

def modulate(xn, shift, scale):
    return xn * (1.0 + scale[:, None, :]) + shift[:, None, :]

def causal_dwconv(x, w, b):
    C = x.shape[-1]
    y = lax.conv_general_dilated(x, w[:, None, :], window_strides=(1,),
                                 padding=[(CONV_K - 1, 0)],
                                 dimension_numbers=('NWC', 'WIO', 'NWC'),
                                 feature_group_count=C)
    return y + b

def gmlp_branch(z_u, z_v, ln_g, ln_b, w_s, b_s):
    u = jax.nn.gelu(z_u)
    v = layernorm(jax.nn.gelu(z_v), ln_g, ln_b)
    B, S, _ = v.shape
    nb = S // GMLP_BLOCK
    v = v.reshape(B, nb, GMLP_BLOCK, GMLP_GROUPS, GMLP_GROUP_DIM)
    cid = jnp.arange(GMLP_BLOCK) // CHUNK
    mask = cid[None, :] <= cid[:, None]
    ws = jnp.where(mask[None], w_s, jnp.zeros_like(w_s))
    mixed = jnp.einsum('gts,bnsgc->bntgc', ws, v) + b_s.T[None, None, :, :, None]
    return u * mixed.reshape(B, S, GMLP_WIDTH)

def mlstm_branch(q, k, v, o_pre, i_pre, f_pre, hn_g):
    out_dtype = q.dtype
    B, S, _ = q.shape
    H, dh, L = MLSTM_HEADS, MLSTM_HEAD_DIM, CHUNK
    nc = S // L

    def heads(t):
        return t.astype(jnp.float32).reshape(B, nc, L, H, dh).transpose(1, 0, 3, 2, 4)

    def gates(t):
        return t.astype(jnp.float32).reshape(B, nc, L, H).transpose(1, 0, 3, 2)

    qh = heads(q) * (dh ** -0.5)
    kh = heads(k)
    vh = heads(v)
    li = gates(i_pre)
    lf = jax.nn.log_sigmoid(gates(f_pre))
    causal = jnp.tril(jnp.ones((L, L), dtype=bool))

    def step(carry, xs):
        C, n, m = carry
        qc, kc, vc, lic, lfc = xs
        bcum = jnp.cumsum(lfc, axis=-1)
        dmat = bcum[..., :, None] - bcum[..., None, :] + lic[..., None, :]
        dmat = jnp.where(causal, dmat, -jnp.inf)
        m_inter = bcum + m[..., None]
        m_t = jnp.maximum(m_inter, jnp.max(dmat, axis=-1))
        wts = jnp.exp(dmat - m_t[..., None])
        s = jnp.einsum('bhtd,bhsd->bhts', qc, kc) * wts
        inter = jnp.exp(m_inter - m_t)
        num = (jnp.einsum('bhts,bhsv->bhtv', s, vc)
               + inter[..., None] * jnp.einsum('bhtk,bhkv->bhtv', qc, C))
        den = jnp.sum(s, axis=-1) + inter * jnp.einsum('bhtk,bhk->bht', qc, n)
        h = num / jnp.maximum(jnp.abs(den), jnp.exp(-m_t))[..., None]
        b_last = bcum[..., -1]
        g = b_last[..., None] - bcum + lic
        m_new = jnp.maximum(b_last + m, jnp.max(g, axis=-1))
        decay = jnp.exp(b_last + m - m_new)
        wk = jnp.exp(g - m_new[..., None])[..., None] * kc
        C = decay[..., None, None] * C + jnp.einsum('bhsk,bhsv->bhkv', wk, vc)
        n = decay[..., None] * n + jnp.sum(wk, axis=2)
        return (C, n, m_new), h

    init = (jnp.zeros((B, H, dh, dh), jnp.float32),
            jnp.zeros((B, H, dh), jnp.float32),
            jnp.zeros((B, H), jnp.float32))
    _, h = lax.scan(step, init, (qh, kh, vh, li, lf))
    h = h.transpose(1, 0, 3, 2, 4).reshape(B, S, H, dh)
    mu = jnp.mean(h, axis=-1, keepdims=True)
    var = jnp.mean(jnp.square(h - mu), axis=-1, keepdims=True)
    h = (h - mu) * lax.rsqrt(var + EPS) * hn_g.astype(jnp.float32).reshape(H, dh)
    h = h.reshape(B, S, MLSTM_WIDTH) * jax.nn.sigmoid(o_pre.astype(jnp.float32))
    return h.astype(out_dtype)

def first_inputs(seed: int = 0) -> dict:
    key = jax.random.key(seed)
    ks = jax.random.split(key, 24)
    f32 = jnp.float32
    D = D_MODEL

    def nrm(k, shape, scale):
        return jax.random.normal(k, shape, f32) * scale

    f_bias = jnp.broadcast_to(jnp.linspace(3.0, 6.0, MLSTM_HEADS, dtype=f32), (DEPTH, MLSTM_HEADS))
    gate_b = jnp.stack([nrm(ks[7], (DEPTH, MLSTM_HEADS), 0.1),
                        f_bias + nrm(ks[8], (DEPTH, MLSTM_HEADS), 0.1)], axis=1)
    return {
        "x": nrm(ks[0], (BATCH, SEQ, D), 1.0),
        "c": nrm(ks[1], (BATCH, D), 1.0),
        "w_ada": nrm(ks[2], (DEPTH, D, 6 * D), 0.5 * D ** -0.5),
        "b_ada": nrm(ks[3], (DEPTH, 6 * D), 0.02),
        "norm1_g": 1.0 + nrm(ks[4], (DEPTH, D), 0.02),
        "w_in": nrm(ks[5], (DEPTH, D, IN_COLS), D ** -0.5),
        "conv_w": nrm(ks[6], (DEPTH, CONV_K, 2 * MLSTM_WIDTH), CONV_K ** -0.5),
        "conv_b": nrm(ks[9], (DEPTH, 2 * MLSTM_WIDTH), 0.02),
        "mlstm_gate_b": gate_b,
        "gmlp_ln_g": 1.0 + nrm(ks[10], (DEPTH, GMLP_WIDTH), 0.02),
        "gmlp_ln_b": nrm(ks[11], (DEPTH, GMLP_WIDTH), 0.02),
        "gmlp_ws": nrm(ks[12], (DEPTH, GMLP_GROUPS, GMLP_BLOCK, GMLP_BLOCK), 0.5 * GMLP_BLOCK ** -0.5),
        "gmlp_bs": 1.0 + nrm(ks[13], (DEPTH, GMLP_GROUPS, GMLP_BLOCK), 0.1),
        "mlstm_hn_g": 1.0 + nrm(ks[14], (DEPTH, MLSTM_WIDTH), 0.02),
        "w_out": nrm(ks[15], (DEPTH, D, D), D ** -0.5),
        "norm2_g": 1.0 + nrm(ks[16], (DEPTH, D), 0.02),
        "w_ff1": nrm(ks[17], (DEPTH, D, FFN_DIM), D ** -0.5),
        "w_ff2": nrm(ks[18], (DEPTH, FFN_DIM, D), FFN_DIM ** -0.5),
        "final_g": 1.0 + nrm(ks[19], (D,), 0.02),
    }

def first_block(x, c, w_ada, b_ada, norm1_g, w_in, conv_w, conv_b, mlstm_gate_b,
              gmlp_ln_g, gmlp_ln_b, gmlp_ws, gmlp_bs, mlstm_hn_g, w_out,
              norm2_g, w_ff1, w_ff2, final_g):
    h = x
    c_act = jax.nn.silu(c)
    for l in range(DEPTH):
        mod = c_act @ w_ada[l] + b_ada[l]
        sh1, sc1, g1, sh2, sc2, g2 = jnp.split(mod, 6, axis=-1)

        xn = modulate(rmsnorm(h, norm1_g[l]), sh1, sc1)
        p = xn @ w_in[l]
        qk = jax.nn.silu(causal_dwconv(p[..., OFF_Q:OFF_MV], conv_w[l], conv_b[l]))
        q, k = jnp.split(qk, 2, axis=-1)
        y_a = gmlp_branch(p[..., OFF_U:OFF_V], p[..., OFF_V:OFF_Q],
                          gmlp_ln_g[l], gmlp_ln_b[l], gmlp_ws[l], gmlp_bs[l])
        y_b = mlstm_branch(q, k, p[..., OFF_MV:OFF_O], p[..., OFF_O:OFF_I],
                           p[..., OFF_I:OFF_F] + mlstm_gate_b[l, 0],
                           p[..., OFF_F:OFF_GA] + mlstm_gate_b[l, 1],
                           mlstm_hn_g[l])
        merged = (jax.nn.sigmoid(p[..., OFF_GA:OFF_GB]) * y_a
                  + jax.nn.sigmoid(p[..., OFF_GB:IN_COLS]) * y_b)
        h = h + g1[:, None, :] * (merged @ w_out[l])

        xn = modulate(rmsnorm(h, norm2_g[l]), sh2, sc2)
        ff = jnp.square(jax.nn.relu(xn @ w_ff1[l])) @ w_ff2[l]
        h = h + g2[:, None, :] * ff
    return rmsnorm(h, final_g)


_first_inputs = first_inputs


def first_inputs(seed=0):
    import zlib

    import numpy as np

    out = dict(_first_inputs(seed))
    spreads = {}
    factors = {'norm1_g': 8.0,
     'conv_b': 64.0,
     'gmlp_ln_g': 35.681,
     'gmlp_ln_b': 33.141,
     'gmlp_bs': 4.535,
     'mlstm_hn_g': 64.0,
     'norm2_g': 18.431,
     'final_g': 8.123,
     'conv_w': 6.234}
    for name, (base, spread) in spreads.items():
        noise = np.random.default_rng([zlib.crc32(name.encode()), seed]).standard_normal(out[name].shape)
        drawn = base * np.exp(spread * noise) if base else spread * noise
        out[name] = __import__('jax').numpy.asarray(drawn.astype(out[name].dtype))
    for name, factor in factors.items():
        out[name] = (out[name] * factor).astype(out[name].dtype)
    return out


_narrow_inputs = first_inputs


def first_inputs(seed=0):

    out = dict(_narrow_inputs(seed))
    wider = {'conv_b': 12.0, 'gmlp_ln_g': 3.35, 'gmlp_ln_b': 3.3, 'mlstm_hn_g': 6.52, 'final_g': 3.21}
    for name, times in wider.items():
        mean = out[name].mean()
        out[name] = (mean + times * (out[name] - mean)).astype(out[name].dtype)
    return out


DEPTH_2 = 2

HEAD_DIM = 64
A_HEADS = 4
DILATED_PATTERNS = ((128, 1), (512, 4), (2048, 16))
WIN_BLOCK = 64
B_HEADS = 8
MLA_Q_LORA = 384
MLA_KV_LORA = 256
MLA_NOPE = 64
MLA_ROPE = 32
MLA_V = 64
ROPE_THETA = 10000.0
C_HEADS = 4
DIFF_QK = 32
DIFF_V = 64
D_FF = 2816
QUERY_BLOCK = 128
NEG_INF = -1e30

A_COLS = 3 * A_HEADS * HEAD_DIM
B_COLS = MLA_Q_LORA + MLA_KV_LORA + MLA_ROPE
C_COLS = 2 * (C_HEADS * 2 * DIFF_QK) + C_HEADS * DIFF_V
N_IN = A_COLS + B_COLS + C_COLS
D_MIX = A_HEADS * HEAD_DIM + B_HEADS * MLA_V + C_HEADS * DIFF_V


def rmsnorm_2(x, gain):
    xf = x.astype(jnp.float32)
    y = xf * lax.rsqrt(jnp.mean(xf * xf, axis=-1, keepdims=True) + EPS)
    return y.astype(x.dtype) * gain

def swiglu(h, w_gate, w_up, w_down):
    return (jax.nn.silu(h @ w_gate) * (h @ w_up)) @ w_down

def alibi_slopes():
    n = A_HEADS + C_HEADS
    s = jnp.asarray([2.0 ** (-8.0 * (i + 1) / n) for i in range(n)], dtype=jnp.float32)
    return s[0::2], s[1::2]

def rope(t, pos):
    half = t.shape[-1] // 2
    inv = ROPE_THETA ** (-jnp.arange(half, dtype=jnp.float32) / half)
    ang = pos.astype(jnp.float32)[..., None, None] * inv
    cos, sin = jnp.cos(ang), jnp.sin(ang)
    tf = t.astype(jnp.float32)
    t1, t2 = tf[..., :half], tf[..., half:]
    return jnp.concatenate([t1 * cos - t2 * sin, t2 * cos + t1 * sin], axis=-1).astype(t.dtype)

def dilated_branch(q, k, v, pos, slopes, dilation, radius):
    B, S, H, E = q.shape
    L = S // dilation

    def to_res(t):
        return t.reshape(B, L, dilation, H, E).transpose(0, 2, 3, 1, 4)

    qr, kr, vr = to_res(q), to_res(k), to_res(v)
    pr = pos.reshape(B, L, dilation).transpose(0, 2, 1)
    nb = -(-L // WIN_BLOCK)
    Lp = nb * WIN_BLOCK
    K = WIN_BLOCK + 2 * radius
    qr = jnp.pad(qr, ((0, 0), (0, 0), (0, 0), (0, Lp - L), (0, 0)))
    kpad = ((0, 0), (0, 0), (0, 0), (radius, radius + Lp - L), (0, 0))
    kr, vr = jnp.pad(kr, kpad), jnp.pad(vr, kpad)
    pq = jnp.pad(pr, ((0, 0), (0, 0), (0, Lp - L)))
    pk = jnp.pad(pr, ((0, 0), (0, 0), (radius, radius + Lp - L)))
    slab = jnp.arange(nb)[:, None] * WIN_BLOCK + jnp.arange(K)[None, :]
    ks = jnp.take(kr, slab, axis=3)
    vs = jnp.take(vr, slab, axis=3)
    pks = jnp.take(pk, slab, axis=2)
    qb = qr.reshape(B, dilation, H, nb, WIN_BLOCK, E)
    pqb = pq.reshape(B, dilation, nb, WIN_BLOCK)
    off = jnp.arange(K)[None, :] - radius - jnp.arange(WIN_BLOCK)[:, None]
    kabs = slab - radius
    valid = (jnp.abs(off) <= radius)[None] & ((kabs >= 0) & (kabs < L))[:, None, :]
    sc = jnp.einsum('bdhnqe,bdhnke->bdhnqk', qb, ks).astype(jnp.float32) * (E ** -0.5)
    dist = jnp.abs(pqb[..., :, None] - pks[..., None, :]).astype(jnp.float32)
    sc = sc - slopes[None, None, :, None, None, None] * dist[:, :, None]
    sc = jnp.where(valid, sc, NEG_INF)
    m = jnp.max(sc, axis=-1)
    p = jnp.exp(sc - m[..., None])
    s = jnp.sum(p, axis=-1)
    o = jnp.einsum('bdhnqk,bdhnke->bdhnqe', p, vs.astype(jnp.float32)) / s[..., None]
    o = o.reshape(B, dilation, H, Lp, E)[:, :, :, :L].transpose(0, 3, 1, 2, 4).reshape(B, S, H, E)
    m = m.reshape(B, dilation, H, Lp)[..., :L].transpose(0, 3, 1, 2).reshape(B, S, H)
    s = s.reshape(B, dilation, H, Lp)[..., :L].transpose(0, 3, 1, 2).reshape(B, S, H)
    return o, m, s

def dilated_attention(q, k, v, pos, slopes):
    outs = [dilated_branch(q, k, v, pos, slopes, d, w // 2 // d) for (w, d) in DILATED_PATTERNS]
    m_all = jnp.max(jnp.stack([m for (_, m, _) in outs]), axis=0)
    wts = [s * jnp.exp(m - m_all) for (_, m, s) in outs]
    num = sum(w[..., None] * o for w, (o, _, _) in zip(wts, outs))
    return num / sum(wts)[..., None]

def mla_attention(q, k, v):
    B, H, S, Dk = q.shape
    nq = S // QUERY_BLOCK
    scale = Dk ** -0.5
    qb = q.reshape(B, H, nq, QUERY_BLOCK, Dk).transpose(2, 0, 1, 3, 4)
    vf = v.astype(jnp.float32)

    def one(qi):
        sc = jnp.einsum('bhqe,bhke->bhqk', qi, k).astype(jnp.float32) * scale
        return jnp.einsum('bhqk,bhkv->bhqv', jax.nn.softmax(sc, axis=-1), vf)

    o = lax.map(one, qb)
    return o.transpose(1, 0, 3, 2, 4).reshape(B, S, H, v.shape[-1])

def diff_attention(q, k, v, pos, slopes, lam):
    B, H, _, S, E = q.shape
    nq = S // QUERY_BLOCK
    scale = E ** -0.5
    qb = q.reshape(B, H, 2, nq, QUERY_BLOCK, E).transpose(3, 0, 1, 2, 4, 5)
    pqb = pos.reshape(B, nq, QUERY_BLOCK).transpose(1, 0, 2)
    vf = v.astype(jnp.float32)

    def one(args):
        qi, pi = args
        sc = jnp.einsum('bhcqe,bhcke->bhcqk', qi, k).astype(jnp.float32) * scale
        dist = jnp.abs(pi[:, :, None] - pos[:, None, :]).astype(jnp.float32)
        sc = sc - slopes[None, :, None, None, None] * dist[:, None, None]
        a = jax.nn.softmax(sc, axis=-1)
        return jnp.einsum('bhqk,bhkv->bhqv', a[:, :, 0] - lam * a[:, :, 1], vf)

    o = lax.map(one, (qb, pqb))
    return o.transpose(1, 0, 3, 2, 4).reshape(B, S, H, v.shape[-1])

def token_mixing(h, pos, w_in, mla_q_norm, mla_w_uq, mla_kv_norm, mla_w_ukv,
                 lq1, lk1, lq2, lk2, diff_head_norm, w_out, layer_idx):
    B, S, _ = h.shape
    slopes_a, slopes_c = alibi_slopes()
    proj = h @ w_in
    a_part, b_part, c_part = jnp.split(proj, [A_COLS, A_COLS + B_COLS], axis=-1)

    qa, ka, va = [t.reshape(B, S, A_HEADS, HEAD_DIM) for t in jnp.split(a_part, 3, axis=-1)]
    out_a = dilated_attention(qa, ka, va, pos, slopes_a).astype(h.dtype)

    c_q, c_kv, k_pe = jnp.split(b_part, [MLA_Q_LORA, MLA_Q_LORA + MLA_KV_LORA], axis=-1)
    qfull = (rmsnorm_2(c_q, mla_q_norm) @ mla_w_uq).reshape(B, S, B_HEADS, MLA_NOPE + MLA_ROPE)
    q_b = jnp.concatenate([qfull[..., :MLA_NOPE], rope(qfull[..., MLA_NOPE:], pos)], axis=-1)
    kv = (rmsnorm_2(c_kv, mla_kv_norm) @ mla_w_ukv).reshape(B, S, B_HEADS, MLA_NOPE + MLA_V)
    k_rot = jnp.broadcast_to(rope(k_pe[:, :, None, :], pos), (B, S, B_HEADS, MLA_ROPE))
    k_b = jnp.concatenate([kv[..., :MLA_NOPE], k_rot], axis=-1)
    v_b = kv[..., MLA_NOPE:]
    out_b = mla_attention(q_b.transpose(0, 2, 1, 3), k_b.transpose(0, 2, 1, 3),
                          v_b.transpose(0, 2, 1, 3)).astype(h.dtype)

    nqk = C_HEADS * 2 * DIFF_QK
    q_c, k_c, v_c = jnp.split(c_part, [nqk, 2 * nqk], axis=-1)
    q_c = q_c.reshape(B, S, C_HEADS, 2, DIFF_QK).transpose(0, 2, 3, 1, 4)
    k_c = k_c.reshape(B, S, C_HEADS, 2, DIFF_QK).transpose(0, 2, 3, 1, 4)
    v_c = v_c.reshape(B, S, C_HEADS, DIFF_V).transpose(0, 2, 1, 3)
    lam_init = 0.8 - 0.6 * math.exp(-0.3 * layer_idx)
    lam = (jnp.exp(jnp.sum(lq1.astype(jnp.float32) * lk1.astype(jnp.float32)))
           - jnp.exp(jnp.sum(lq2.astype(jnp.float32) * lk2.astype(jnp.float32))) + lam_init)
    o_c = diff_attention(q_c, k_c, v_c, pos, slopes_c, lam).astype(h.dtype)
    out_c = rmsnorm_2(o_c, diff_head_norm) * (1.0 - lam_init)

    mixed = jnp.concatenate([out_a.reshape(B, S, -1), out_b.reshape(B, S, -1),
                             out_c.reshape(B, S, -1)], axis=-1)
    return mixed @ w_out

def second_inputs(seed: int = 0) -> dict:
    key = jax.random.key(seed)
    ks = iter(jax.random.split(key, 32))
    f32 = jnp.float32

    def dense(shape, fan_in):
        return jax.random.normal(next(ks), shape, f32) * (fan_in ** -0.5)

    def gain(shape):
        return 1.0 + 0.02 * jax.random.normal(next(ks), shape, f32)

    return {
        "x": jax.random.normal(next(ks), (BATCH, SEQ, D_MODEL), f32),
        "positions": jnp.broadcast_to(jnp.arange(SEQ, dtype=jnp.int32), (BATCH, SEQ)),
        "ffn1_norm": gain((DEPTH_2, D_MODEL)),
        "ffn1_w_gate": dense((DEPTH_2, D_MODEL, D_FF), D_MODEL),
        "ffn1_w_up": dense((DEPTH_2, D_MODEL, D_FF), D_MODEL),
        "ffn1_w_down": dense((DEPTH_2, D_FF, D_MODEL), D_FF),
        "mix_norm": gain((DEPTH_2, D_MODEL)),
        "w_in": dense((DEPTH_2, D_MODEL, N_IN), D_MODEL),
        "mla_q_norm": gain((DEPTH_2, MLA_Q_LORA)),
        "mla_w_uq": dense((DEPTH_2, MLA_Q_LORA, B_HEADS * (MLA_NOPE + MLA_ROPE)), MLA_Q_LORA),
        "mla_kv_norm": gain((DEPTH_2, MLA_KV_LORA)),
        "mla_w_ukv": dense((DEPTH_2, MLA_KV_LORA, B_HEADS * (MLA_NOPE + MLA_V)), MLA_KV_LORA),
        "diff_lambda_q1": 0.1 * jax.random.normal(next(ks), (DEPTH_2, DIFF_QK), f32),
        "diff_lambda_k1": 0.1 * jax.random.normal(next(ks), (DEPTH_2, DIFF_QK), f32),
        "diff_lambda_q2": 0.1 * jax.random.normal(next(ks), (DEPTH_2, DIFF_QK), f32),
        "diff_lambda_k2": 0.1 * jax.random.normal(next(ks), (DEPTH_2, DIFF_QK), f32),
        "diff_head_norm": gain((DEPTH_2, DIFF_V)),
        "w_out": dense((DEPTH_2, D_MIX, D_MODEL), D_MIX),
        "ffn2_norm": gain((DEPTH_2, D_MODEL)),
        "ffn2_w_gate": dense((DEPTH_2, D_MODEL, D_FF), D_MODEL),
        "ffn2_w_up": dense((DEPTH_2, D_MODEL, D_FF), D_MODEL),
        "ffn2_w_down": dense((DEPTH_2, D_FF, D_MODEL), D_FF),
        "final_norm": gain((D_MODEL,)),
    }

def second_block(x, positions, ffn1_norm, ffn1_w_gate, ffn1_w_up, ffn1_w_down, mix_norm, w_in,
              mla_q_norm, mla_w_uq, mla_kv_norm, mla_w_ukv, diff_lambda_q1, diff_lambda_k1,
              diff_lambda_q2, diff_lambda_k2, diff_head_norm, w_out, ffn2_norm, ffn2_w_gate,
              ffn2_w_up, ffn2_w_down, final_norm):
    for l in range(DEPTH_2):
        x = x + 0.5 * swiglu(rmsnorm_2(x, ffn1_norm[l]), ffn1_w_gate[l], ffn1_w_up[l], ffn1_w_down[l])
        x = x + token_mixing(rmsnorm_2(x, mix_norm[l]), positions, w_in[l], mla_q_norm[l], mla_w_uq[l],
                             mla_kv_norm[l], mla_w_ukv[l], diff_lambda_q1[l], diff_lambda_k1[l],
                             diff_lambda_q2[l], diff_lambda_k2[l], diff_head_norm[l], w_out[l], l)
        x = x + 0.5 * swiglu(rmsnorm_2(x, ffn2_norm[l]), ffn2_w_gate[l], ffn2_w_up[l], ffn2_w_down[l])
    return rmsnorm_2(x, final_norm)


def setup_inputs(seed=0):
    out = dict(first_inputs(seed))
    for name, value in second_inputs(seed + 1).items():
        if name != "x":
            out[name + "_2"] = value
    return out


def reference(
    x, c, w_ada, b_ada, norm1_g, w_in, conv_w, conv_b, mlstm_gate_b, gmlp_ln_g, gmlp_ln_b,
    gmlp_ws, gmlp_bs, mlstm_hn_g, w_out, norm2_g, w_ff1, w_ff2, final_g, positions_2,
    ffn1_norm_2, ffn1_w_gate_2, ffn1_w_up_2, ffn1_w_down_2, mix_norm_2, w_in_2, mla_q_norm_2,
    mla_w_uq_2, mla_kv_norm_2, mla_w_ukv_2, diff_lambda_q1_2, diff_lambda_k1_2,
    diff_lambda_q2_2, diff_lambda_k2_2, diff_head_norm_2, w_out_2, ffn2_norm_2, ffn2_w_gate_2,
    ffn2_w_up_2, ffn2_w_down_2, final_norm_2,
):
    x = first_block(
        x, c, w_ada, b_ada, norm1_g, w_in, conv_w, conv_b, mlstm_gate_b, gmlp_ln_g, gmlp_ln_b,
        gmlp_ws, gmlp_bs, mlstm_hn_g, w_out, norm2_g, w_ff1, w_ff2, final_g,
    )
    return second_block(
        x, positions_2, ffn1_norm_2, ffn1_w_gate_2, ffn1_w_up_2, ffn1_w_down_2, mix_norm_2,
        w_in_2, mla_q_norm_2, mla_w_uq_2, mla_kv_norm_2, mla_w_ukv_2, diff_lambda_q1_2,
        diff_lambda_k1_2, diff_lambda_q2_2, diff_lambda_k2_2, diff_head_norm_2, w_out_2,
        ffn2_norm_2, ffn2_w_gate_2, ffn2_w_up_2, ffn2_w_down_2, final_norm_2,
    )


_drawn_inputs = setup_inputs


def setup_inputs(seed=0):
    import zlib

    import numpy as np

    out = dict(_drawn_inputs(seed))
    spreads = {}
    factors = {'conv_b': 6.487,
     'ffn1_norm_2': 8.0,
     'mix_norm_2': 8.0,
     'mla_q_norm_2': 8.0,
     'mla_w_uq_2': 5.788,
     'mla_kv_norm_2': 8.0,
     'diff_lambda_q1_2': 8.0,
     'diff_lambda_k1_2': 8.0,
     'diff_lambda_q2_2': 8.0,
     'diff_lambda_k2_2': 8.0,
     'diff_head_norm_2': 41.789,
     'ffn2_norm_2': 8.0,
     'final_norm_2': 8.061}
    for name, (base, spread) in spreads.items():
        noise = np.random.default_rng([zlib.crc32(name.encode()), seed]).standard_normal(out[name].shape)
        drawn = base * np.exp(spread * noise) if base else spread * noise
        out[name] = __import__('jax').numpy.asarray(drawn.astype(out[name].dtype))
    for name, factor in factors.items():
        out[name] = (out[name] * factor).astype(out[name].dtype)
    return out
```

```python
import math
from contextlib import ExitStack

import numpy as np

import concourse.bass as bass
from concourse import mybir

F32 = mybir.dt.float32
I32 = mybir.dt.int32
ACT = mybir.ActivationFunctionType
ALU = mybir.AluOpType
AX_X = mybir.AxisListType.X

P = 128
S = 512
ST = S // P
D = 1024
DT = D // P
EPS = 1e-6
TWO_PI = 2.0 * math.pi

HEADS = 4
HEAD_DIM = 256
VT = HEAD_DIM // P
GROUPS = 8
CONV_K = 4
FF_TILES = 4 * D // P

LAYERS = 2
F_TILES = 2816 // P
A_HEADS, B_HEADS, C_HEADS = 4, 8, 4
NOPE, ROPE = 64, 32
Q_TILES, KV_TILES = 3, 2
SCALE_A = 64.0**-0.5
SCALE_B = (NOPE + ROPE) ** -0.5
SCALE_C = 32.0**-0.5
N_SLOPES = A_HEADS + C_HEADS
SLOPES = [2.0 ** (-8.0 * (i + 1) / N_SLOPES) for i in range(N_SLOPES)]
LAMBDA_INIT = [0.8 - 0.6 * math.exp(-0.3 * layer) for layer in range(LAYERS)]
WINDOW_PATTERNS = ((128, 1), (512, 4), (2048, 16))

RING = 4
SLOT_UNITS = F_TILES
BANKS = 4
UNIT = P

CHUNKS_1 = [("ada", 24), ("v", 4), ("u", 4), ("ga", 4), ("qk", 8), ("mv", 4), ("o", 4), ("gb", 4),
            ("out1", 4), ("ff1", 16), ("ff2", 16)]
TILES_1 = [("ada", 24), ("v", 8), ("u", 8), ("mix", 8), ("ga", 8), ("qk", 16), ("mv", 8), ("o", 8),
           ("gb", 8), ("cell", 16), ("out1", 8), ("ff1", 32), ("ff2", 8)]
CHUNKS_2 = [("up_a", 22), ("down_a", 8), ("in", 7), ("in_v", 2), ("uq", 2), ("ukv", 1), ("out2", 4),
            ("up_b", 22), ("down_b", 8)]
TILES_2 = [("up_a", 44), ("down_a", 8), ("in", 14), ("in_v", 4), ("uq", 6), ("uk", 4), ("uv", 4),
           ("out2", 8), ("up_b", 44), ("down_b", 8)]
LAYER_CHUNKS = sum(n for _, n in CHUNKS_2)
LAYER_TILES = sum(n for _, n in TILES_2)
assert LAYER_CHUNKS % RING == 0 and LAYER_TILES % BANKS == 0

SHAPES = {"u": (8, 16, 8, 8), "ga": (8, 16, 8, 8), "qk": (8, 16, 16, 8), "o": (8, 16, 8, 8),
          "gb": (8, 16, 8, 8), "out1": (8, 16, 8, 8), "ff1": (8, 16, 32, 8), "ff2": (32, 16, 8, 4),
          "up_a": (8, 16, 44, 8), "up_b": (8, 16, 44, 8), "down_a": (22, 22, 8, 4),
          "down_b": (22, 22, 8, 4), "in": (8, 16, 14, 8), "uq": (3, 9, 6, 6), "out2": (8, 16, 8, 8)}


def starts(first, second):
    at, found = 0, {}
    for name, n in first + second:
        found[name] = at
        at += n
    return found


CHUNK0 = starts(CHUNKS_1, CHUNKS_2)
TILE0 = starts(TILES_1, TILES_2)
IN_LAYER = {name for name, _ in CHUNKS_2 + TILES_2}

COLS_1 = [("c", 8), ("b_ada", 48), ("norm1", 8), ("conv_w", 64), ("conv_b", 16), ("ln_g", 8),
          ("ln_b", 8), ("hn_g", 8), ("norm2", 8), ("final1", 8), ("final2", 8), ("inv_freq", 1),
          ("sin_sign", 1)]
COL1 = starts(COLS_1, [])
N_COLS_1 = sum(n for _, n in COLS_1)
COLS_2 = [("ffn_a", 8), ("mix", 8), ("qn", 3), ("kvn", 2), ("ffn_b", 8), ("head", 1), ("neg_lam", 1)]
COL2 = starts(COLS_2, [])
N_COLS_2 = sum(n for _, n in COLS_2)
N_COLS = N_COLS_1 + LAYERS * N_COLS_2

IDENT, SWAP, ONES, MEAN256, HEAD_ONES = range(5)
N_CONSTS = 5

MAPS = ([("A", h, 0) for h in range(A_HEADS)] + [("B", h, 0) for h in range(B_HEADS)]
        + [("C", h, c) for h in range(C_HEADS) for c in range(2)])
OUTPUTS = [m for m, (kind, _, c) in enumerate(MAPS) if kind != "C" or c == 1]
DVE_READ = [m for m, (kind, _, _) in enumerate(MAPS) if kind != "B"]


def sequence(scores_first):
    order = [("scores", 0), ("scores", 1)]
    for m in range(len(MAPS)):
        steps = [("output", m)] if m in OUTPUTS else []
        ahead = [("scores", m + 2)] if m + 2 < len(MAPS) else []
        order += ahead + steps if scores_first else steps + ahead
    return order


PE_ORDER, SOFT_ORDER = sequence(True), sequence(False)

Q_IN, KV_IN, PE_IN, QC_IN, KC_IN, QA_IN, KA_IN = 0, 3, 5, 6, 8, 10, 12


def build(nc: bass.Bass, A: dict, out: bass.AP):
    with ExitStack() as ctx:
        names = {}

        def sb(name, shape, dtype=F32):
            return ctx.enter_context(nc.sbuf_tensor(name, shape, dtype))

        def sem(name):
            if name not in names:
                names[name] = ctx.enter_context(nc.semaphore(name))
            return names[name]

        h = sb("h", [P, DT, S])
        xn = sb("xn", [P, DT, S])
        mixed = xn
        ring = sb("ring", [P, RING, SLOT_UNITS * UNIT])
        cols = sb("cols", [P, N_COLS])
        lcols = sb("lcols", [P, N_COLS_2])
        consts = sb("consts_sb", [P, N_CONSTS, P])
        stat = sb("stat", [P, 64])
        mod = sb("mod", [P, 48])
        arena = sb("arena", [P, 30720])
        ps = ctx.enter_context(nc.psum_tensor("ps", [P, 8, S], F32))
        ident, swap, ones = consts[:, IDENT, :], consts[:, SWAP, :], consts[:, ONES, :]

        def part(at, tiles, width=S):
            return arena[:, at:at + tiles * width].rearrange("p (t s) -> p t s", t=tiles)

        merged = part(0, 8)
        qf = part(4096, 8)
        kf = part(8192, 8)
        mv = part(12288, 4, D)
        so = part(16384, 8)
        tmp = part(20480, 4)
        neg_m = part(22528, 4)
        e_mt = part(24576, 4)
        cell_s = part(26624, 4)
        cell_w = part(28672, 4)
        v_tok = part(4096, 4, D)
        gu = kf
        ws_t = part(12288, GROUPS, P)
        bs_row = part(13312, GROUPS, P)
        mix_base = part(14336, GROUPS, P)
        hid1 = part(0, FF_TILES)
        rows = arena[0:4, 26624:26624 + 8 * S].rearrange("p (t s) -> p t s", t=8)
        wif = sb("wif", [P, DT, 36])
        gate_b = sb("gate_b", [4, 2])
        cact = stat[:, 0:8]
        gain1 = stat[:, 8:16]
        gain2 = stat[:, 16:24]
        a_col = stat[:, 24:40].rearrange("p (t h) -> p t h", t=ST)
        ssq = sb("ssq", [P, S])
        nrm = sb("nrm", [P, 3, ST])
        bn = sb("bn", [P, ST, 2, 6])
        bn_mv = sb("bn_mv", [P, ST, 2])
        hid2 = part(0, F_TILES)
        proj = part(0, 14)
        v_ac = part(7168, ST)
        qb = part(9216, 4)
        qr = part(11264, 2)
        kb = part(12288, 4)
        v_b = part(14336, ST)
        probs = [part(16384, ST), part(18432, ST)]
        probs_t = part(20480, ST)
        bias_a = proj[:, 0:ST, :]
        dist = part(22528, ST)
        log_c = part(24576, ST)
        cos_t = arena[:, 26624:27136]
        sin_t = arena[:, 27136:27648]
        tmp2 = part(27648, 4)
        probs.append(tmp2)
        lam_in = sb("lam_in", [P, LAYERS, 4, 32])
        lam_w = sb("lam_w", [P, 32])
        lam_s = sb("lam_s", [P, 4])
        pos_i = sb("pos_i", [P, S + ST], I32)
        soft = sb("soft", [P, 3, 4, ST])
        mx, neg_mx, rsum, rinv = range(4)

        def chunk(name, c, it, per_it, layer):
            at = CHUNK0[name] + c
            return at % RING, at // RING + it * (per_it // RING) + layer * (LAYER_CHUNKS // RING)

        def bank(name, t, it, per_it, layer):
            at = TILE0[name] + t
            return at % BANKS, at // BANKS + it * (per_it // BANKS) + layer * (LAYER_TILES // BANKS)

        def wait(eng, name, value):
            if not (isinstance(value, int) and value <= 0):
                eng.wait_ge(sem(name), value)

        def wait_chunk(pe, name, c, it=0, per_it=0, layer=0):
            slot, before = chunk(name, c, it, per_it, layer)
            pe.wait_ge(sem(f"landed{slot}"), 16 * before + 16)

        def wait_bank(pe, name, t, it=0, per_it=0, layer=0):
            b, before = bank(name, t, it, per_it, layer)
            wait(pe, f"evacuated{b}", before)

        def wait_evacuated(eng, name, t, it=0, per_it=0, layer=0):
            b, before = bank(name, t, it, per_it, layer)
            eng.wait_ge(sem(f"evacuated{b}"), before + 1)

        def evacuated_count(name, t, layer=0):
            b, before = bank(name, t, 0, 0, layer)
            return sem(f"evacuated{b}"), before + 1

        def evacuated(name, t):
            return sem(f"evacuated{(TILE0[name] + t) % BANKS}")

        def bank_ap(name, t):
            return ps[:, (TILE0[name] + t) % BANKS, :]

        def steps(eng, total, per_body, body, peel=0):
            full = total // per_body
            for it in range(peel):
                body(it, range(per_body))
            if full - peel > 1:
                with eng.Fori(peel, full) as it:
                    body(it, range(per_body))
            elif full - peel == 1:
                body(peel, range(per_body))
            if total % per_body:
                body(full, range(total % per_body))

        def wait_tile(eng, name, u, it=0, layer=0):
            K, upc, total, per = SHAPES[name]
            it, u = it + u // per, u % per
            unit = u * K + K - 1
            if (unit + 1) % upc == 0:
                slot, before = chunk(name, unit // upc, it, per * K // upc, layer)
                eng.wait_ge(sem(f"used{slot}"), before + 1)
            else:
                mids = [x for x in range(per) if (x * K + K) % upc]
                all_mids = sum(1 for x in range(total) if (x * K + K) % upc)
                eng.wait_ge(sem(f"{name}_tile"), mids.index(u) + 1 + it * len(mids) + layer * all_mids)

        def pe_product(pe, name, moving, layer=0, ready=None):
            K, upc, total, per = SHAPES[name]
            per_chunks = per * K // upc

            def body(it, places):
                for u in places:
                    for k in range(K):
                        unit = u * K + k
                        if unit % upc == 0:
                            wait_chunk(pe, name, unit // upc, it, per_chunks, layer)
                        if k == 0:
                            wait_bank(pe, name, u, it, per, layer)
                        if ready is not None and u == 0:
                            pe.wait_ge(*ready(k))
                        slot = (CHUNK0[name] + unit // upc) % RING
                        w = ring[:, slot, (unit % upc) * UNIT:(unit % upc + 1) * UNIT]
                        mm = nc.tensor.matmul(bank_ap(name, u), w, moving(k), start=(k == 0), stop=(k == K - 1))
                        if (unit + 1) % upc == 0:
                            mm.then_inc(sem(f"used{slot}"), 1)
                        elif k == K - 1:
                            mm.then_inc(sem(f"{name}_tile"), 1)

            steps(nc.tensor, total, per, body)

        def pe_token_product(pe, name, half, tile_base, layer=0):
            for c in range(2):
                wait_chunk(pe, name, 2 * half + c, layer=layer)
            for st in range(ST):
                wait_bank(pe, name, tile_base + st, layer=layer)
                for k in range(DT):
                    slot = (CHUNK0[name] + 2 * half + k // 4) % RING
                    w = ring[:, slot, (k % 4) * S:(k % 4 + 1) * S]
                    mm = nc.tensor.matmul(bank_ap(name, tile_base + st), xn[:, k, st * P:(st + 1) * P], w,
                                          start=(k == 0), stop=(k == DT - 1))
                    if st == ST - 1 and k % 4 == 3:
                        mm.then_inc(sem(f"used{slot}"), 1)
                    elif k == DT - 1:
                        mm.then_inc(sem(f"{name}_tile"), 1)

        def wait_token_tile(eng, name, half, st, layer=0, halves=2):
            if st == ST - 1:
                slot, before = chunk(name, 2 * half + 1, 0, 0, layer)
                eng.wait_ge(sem(f"used{slot}"), before + 1)
            else:
                eng.wait_ge(sem(f"{name}_tile"), 3 * half + st + 1 + layer * 3 * halves)

        SQUARES = [0, 8, 16]
        SQ_LAYER = [0, 8, 16, 19, 21]
        SQ_PER_LAYER = 29

        def norm_at(j, layer):
            return (j, SQUARES[j]) if j < 3 else (j + 5 * layer, 24 + SQ_LAYER[j - 3] + SQ_PER_LAYER * layer)

        N_LAST = 3 + 5 * LAYERS

        def sq_parity(j, t):
            return ((SQUARES[j] if j < 3 else 24 + SQ_LAYER[j - 3] if j < 8 else 0) + t) % 2

        def act_square(act, q, slot_buf, src):
            wait(act, "sq_added", q - 1)
            nc.scalar.activation(slot_buf, src, ACT.Square).then_inc(sem("sq_made"), 1)

        def dve_add_square(dve, q, slot_buf):
            dve.wait_ge(sem("sq_made"), q + 1)
            nc.vector.tensor_tensor(ssq[:, :], ssq[:, :], slot_buf, ALU.add).then_inc(sem("sq_added"), 1)
            dve.drain()

        def pe_norm(pe, n, last_square):
            pe.wait_ge(sem("sq_added"), last_square)
            for st in range(ST):
                mm = nc.tensor.matmul(ps[:, 7, st:st + 1], ssq[:, st * P:(st + 1) * P], ones[:, 0:1],
                                      start=True, stop=True)
            mm.then_inc(sem("nrm_sum"), 1)
            pe.wait_ge(sem("nrm_diag"), n + 1)
            nc.tensor.matmul(ps[:, 6, :], ones, ssq[:, :], start=True, stop=True).then_inc(sem("nrm_scale"), 1)

        def dve_norm(dve, n, width):
            dve.wait_ge(sem("nrm_sum"), n + 1)
            nc.vector.tensor_scalar(nrm[:, 0, :], ps[:, 7, 0:ST], 1.0 / width, EPS, ALU.mult, ALU.add)
            dve.drain()
            nc.vector.reciprocal(nrm[:, 1, :], nrm[:, 0, :]).then_inc(sem("nrm_recip"), 1)
            dve.wait_ge(sem("nrm_root"), n + 1)
            for st in range(ST):
                last = nc.vector.tensor_scalar(ssq[:, st * P:(st + 1) * P], ident, nrm[:, 2, st:st + 1], None,
                                               ALU.mult)
            last.then_inc(sem("nrm_diag"), 1)
            dve.wait_ge(sem("nrm_scale"), n + 1)
            nc.vector.memset(ssq[:, :], 0.0)
            dve.drain()

        def act_norm(act, n):
            act.wait_ge(sem("nrm_recip"), n + 1)
            nc.scalar.activation(nrm[:, 2, :], nrm[:, 1, :], ACT.Sqrt).then_inc(sem("nrm_root"), 1)

        def scaled(dve, dst, src, gain, name):
            nc.vector.scalar_tensor_tensor(dst, src, gain, ps[:, 6, :], ALU.mult, ALU.mult)\
                .then_inc(sem(name), 1)

        block = ctx.enter_context(nc.Block())

        @block.sync
        def _(sp):
            def load(name, src, units, total, per, layer=0):
                n_all = total

                def body(it, places):
                    for c in places:
                        slot, before = chunk(name, c, it, per, layer)
                        wait(sp, f"used{slot}", before)
                        nc.sync.dma_start(ring[:, slot, 0:units * UNIT], src[layer * n_all + it * per + c, :, :])\
                            .then_inc(sem(f"landed{slot}"), 16)

                steps(nc.sync, total, per, body, peel=int(name == "ada"))

            def load_one(name, src, units, total, layer):
                for c in range(total):
                    slot, before = chunk(name, c, 0, 0, layer)
                    wait(sp, f"used{slot}", before)
                    nc.sync.dma_start(ring[:, slot, 0:units * UNIT], src[layer * total + c, :, :])\
                        .then_inc(sem(f"landed{slot}"), 16)

            load("ada", A["w_ada"], 16, 24, 4)
            for name, n in CHUNKS_1[1:]:
                if n > 4:
                    load(name, A["w_" + name], 16, n, 8 if name == "ff2" else 4)
                else:
                    load_one(name, A["w_" + name], 16, n, 0)
            with nc.sync.Fori(0, LAYERS) as layer:
                load("up_a", A["w_up_a"], 16, 22, 4, layer)
                load("down_a", A["w_down_a"], 22, 8, 4, layer)
                load_one("in", A["w_in2"], 16, 7, layer)
                load_one("in_v", A["w_in_v"], 16, 2, layer)
                load_one("uq", A["w_uq"], 9, 2, layer)
                load_one("ukv", A["w_ukv"], 16, 1, layer)
                load_one("out2", A["w_out2"], 16, 4, layer)
                load("up_b", A["w_up_b"], 16, 22, 4, layer)
                load("down_b", A["w_down_b"], 22, 8, 4, layer)
            sp.wait_ge(sem("result"), DT)
            nc.sync.dma_start(out, h[:, :, :]).then_inc(sem("stored"), 16)
            sp.wait_ge(sem("stored"), 16)

        @block.gpsimd
        def _(pool):
            nc.gpsimd.dma_start(cols[:, :], A["cols"]).then_inc(sem("in_cols"), 16)
            nc.gpsimd.dma_start(consts[:, :, :], A["consts"]).then_inc(sem("in_consts"), 16)
            nc.gpsimd.dma_start(h[:, :, :], A["x"]).then_inc(sem("in_x"), 16)
            nc.gpsimd.dma_start(wif[:, :, :], A["w_if"]).then_inc(sem("in_gates"), 16)
            nc.gpsimd.dma_start(gate_b[:, :], A["gate_b"]).then_inc(sem("in_gates"), 16)
            nc.gpsimd.dma_start(ws_t, A["ws_t"]).then_inc(sem("in_mix"), 16)
            nc.gpsimd.dma_start(bs_row, A["bs_row"]).then_inc(sem("in_mix"), 16)
            nc.gpsimd.dma_start(lam_in[:, :, :, :], A["lam"]).then_inc(sem("in_lam"), 16)
            nc.gpsimd.dma_start(pos_i[:, :], A["pos"]).then_inc(sem("in_pos"), 16)
            pool.wait_ge(sem("in_mix"), 32)
            nc.gpsimd.memset(ws_t[P // 2:P, :, 0:P // 2], 0.0).then_inc(sem("ws_masked"), 1)
            for hd in range(HEADS):
                for j in range(ST):
                    pool.wait_ge(sem("cell_exp"), ST * hd + j + 1)
                    nc.gpsimd.affine_select(out=cell_w[:, j, 0:P], in_=cell_w[:, j, 0:P],
                                            compare_op=ALU.is_ge, fill=0.0, base=0,
                                            pattern=[[1, P]], channel_multiplier=-1)\
                        .then_inc(sem("cell_masked"), 1)
            pool.wait_ge(sem("block1"), DT)
            nc.gpsimd.dma_start(log_c, A["log_c"]).then_inc(sem("in_log_c"), 16)

        @block.tensor
        def _(pe):
            pe.wait_ge(sem("in_consts"), 16)
            pe.wait_ge(sem("cact"), 1)

            def ada(it, places):
                for c in places:
                    wait_chunk(pe, "ada", c, it, 4)
                    wait_bank(pe, "ada", c, it, 4)
                    for n in range(2):
                        for k in range(DT):
                            w = ring[:, c, (n * DT + k) * UNIT:(n * DT + k + 1) * UNIT]
                            mm = nc.tensor.matmul(bank_ap("ada", c)[:, n:n + 1], w, cact[:, k:k + 1],
                                                  start=(k == 0), stop=(k == DT - 1))
                    mm.then_inc(sem(f"used{c}"), 1)

            steps(nc.tensor, 24, 4, ada, peel=1)
            pe_norm(pe, 0, 8)

            pe.wait_ge(sem("in_gates"), 32)
            for k in range(DT):
                pe.wait_ge(sem("xn1"), k + 1)
                mm = nc.tensor.matmul(ps[0:36, 5, :], wif[:, k, :], xn[:, k, :], start=(k == 0), stop=(k == DT - 1))
            mm.then_inc(sem("gates_made"), 1)
            for half in range(2):
                pe_token_product(pe, "v", half, ST * half)
            pe_product(pe, "u", lambda k: xn[:, k, :])
            pe.wait_ge(sem("ws_masked"), 1)
            for half in range(2):
                wait(pe, "ws_base", 4 * half)
                nc.tensor.matmul(ps[:, 4, :], ones, ws_t[:, 4 * half:4 * half + 4, :], start=True, stop=True)\
                    .then_inc(sem("ws_sums"), 1)
            for g in range(GROUPS):
                wait_bank(pe, "mix", g)
                pe.wait_ge(sem("v_normed"), ST)
                for nb in range(ST):
                    mm = nc.tensor.matmul(bank_ap("mix", g)[:, nb * P:(nb + 1) * P], v_tok[:, nb, g * P:(g + 1) * P],
                                          ws_t[:, g, :], start=True, stop=True)
                mm.then_inc(sem("mix_tile"), 1)
            pe_product(pe, "ga", lambda k: xn[:, k, :])
            pe.wait_ge(sem("rows_ready"), 1)
            for st in range(ST):
                mm = nc.tensor.matmul(ps[:, 7, st * HEADS:(st + 1) * HEADS], rows[:, 2, st * P:(st + 1) * P],
                                      ident[0:HEADS, 0:HEADS], start=True, stop=True)
            mm.then_inc(sem("a_cols"), 1)
            for n in range(2 * HEADS):
                hd, which = n // 2, n % 2
                wait(pe, "spread_read", n - 1)
                pick = consts[0:HEADS, IDENT, hd:hd + 1].to_broadcast([HEADS, P])
                nc.tensor.matmul(ps[:, 4 + which, :], pick, rows[:, 4 + which, :], start=True, stop=True)\
                    .then_inc(sem("spread"), 1)
            pe_product(pe, "qk", lambda k: xn[:, k, :])
            for half in range(2):
                pe_token_product(pe, "mv", half, ST * half)
            pe_product(pe, "o", lambda k: xn[:, k, :])
            pe_product(pe, "gb", lambda k: xn[:, k, :])

            pe.wait_ge(sem("qk_silu"), 16)

            def cell_scores(hd):
                for j in range(ST):
                    t = ST * hd + j
                    wait_bank(pe, "cell", t)
                    for v in range(VT):
                        mm = nc.tensor.matmul(bank_ap("cell", t)[:, 0:S - j * P],
                                              kf[:, VT * hd + v, j * P:(j + 1) * P],
                                              qf[:, VT * hd + v, j * P:S], start=(v == 0), stop=(v == VT - 1))
                    mm.then_inc(sem("cell_tile"), 1)

            def cell_sums(hd):
                wait(pe, "cell_h", VT * hd)
                for v in range(VT + 1):
                    for j in range(ST):
                        if v == 0:
                            wait_evacuated(pe, "cell", ST * hd + j)
                        w = mv[:, j, hd * HEAD_DIM + v * P:hd * HEAD_DIM + (v + 1) * P] if v < VT else ones
                        mm = nc.tensor.matmul(ps[:, 4 + v, j * P:S], w, cell_s[:, j, 0:S - j * P],
                                              start=(j == 0), stop=(j == ST - 1))
                mm.then_inc(sem("cell_sums"), 1)

            def cell_norm(hd):
                mean = consts[:, MEAN256, :]
                pe.wait_ge(sem("cell_h"), VT * hd + VT)
                wait(pe, "cell_var_read", hd)
                for v in range(VT):
                    mm = nc.tensor.matmul(ps[:, 7, :], mean, qf[:, VT * hd + v, :], start=(v == 0), stop=(v == VT - 1))
                mm.then_inc(sem("cell_mean"), 1)
                pe.wait_ge(sem("cell_sq"), VT * hd + VT)
                for v in range(VT):
                    mm = nc.tensor.matmul(ps[:, 7, :], mean, tmp[:, v, :], start=(v == 0), stop=(v == VT - 1))
                mm.then_inc(sem("cell_var"), 1)

            for t in range(ST, 2 * ST):
                wait_evacuated(pe, "mv", t)
            cell_scores(0)
            for hd in range(HEADS):
                if hd + 1 < HEADS:
                    cell_scores(hd + 1)
                cell_sums(hd)
                cell_norm(hd)
            pe.wait_ge(sem("merged_ready"), DT)
            pe_product(pe, "out1", lambda k: merged[:, k, :])
            pe_norm(pe, 1, 16)
            pe.wait_ge(sem("xn2"), DT)
            pe_product(pe, "ff1", lambda k: xn[:, k, :])
            pe.wait_ge(sem("ff1_squared3"), FF_TILES // 4)
            pe_product(pe, "ff2", lambda k: hid1[:, k, :])
            pe_norm(pe, 2, 24)

            def ffn(name, down, normed, n, last_sq, layer):
                pe_norm(pe, n, last_sq)
                pe_product(pe, name, lambda k: xn[:, k, :], layer, lambda k: (sem(normed), DT * layer + k + 1))
                pe_product(pe, down, lambda k: hid2[:, k, :], layer,
                           lambda k: evacuated_count(name, 2 * F_TILES - 1, layer))

            with nc.tensor.Fori(0, LAYERS) as layer:
                n, q = norm_at(3, layer)
                ffn("up_a", "down_a", "xn_a", n, q + 8, layer)
                n, q = norm_at(4, layer)
                pe_norm(pe, n, q + 8)
                pe_product(pe, "in", lambda k: xn[:, k, :], layer, lambda k: (sem("xn_m"), DT * layer + k + 1))
                pe_token_product(pe, "in_v", 0, 0, layer)
                wait_evacuated(pe, "in", 13, layer=layer)
                wait_evacuated(pe, "in", 12, layer=layer)
                nc.tensor.matmul(ps[:, 5, :], swap, proj[:, PE_IN, :], start=True, stop=True)\
                    .then_inc(sem("swapped"), 1)
                for j, count in ((5, 3), (6, 2)):
                    n, q = norm_at(j, layer)
                    if j == 6:
                        pe.wait_ge(sem("q_normed"), Q_TILES * layer + Q_TILES)
                    pe_norm(pe, n, q + count)
                pe_product(pe, "uq", lambda k: proj[:, Q_IN + k, :], layer)
                pe.wait_ge(sem("kv_normed"), KV_TILES * layer + KV_TILES)
                wait_chunk(pe, "ukv", 0, layer=layer)
                slot = CHUNK0["ukv"] % RING
                for t in range(4):
                    wait_bank(pe, "uk", t, layer=layer)
                    for k in range(KV_TILES):
                        w = ring[:, slot, (t * KV_TILES + k) * UNIT:(t * KV_TILES + k + 1) * UNIT]
                        mm = nc.tensor.matmul(bank_ap("uk", t), w, proj[:, KV_IN + k, :], start=(k == 0),
                                              stop=(k == KV_TILES - 1))
                    mm.then_inc(sem("uk_tile"), 1)
                for t in range(ST):
                    wait_bank(pe, "uv", t, layer=layer)
                    for k in range(KV_TILES):
                        w = ring[:, slot, (8 + 4 * k) * UNIT:(12 + 4 * k) * UNIT]
                        mm = nc.tensor.matmul(bank_ap("uv", t), proj[:, KV_IN + k, t * P:(t + 1) * P], w,
                                              start=(k == 0), stop=(k == KV_TILES - 1))
                    mm.then_inc(sem("uv_tile" if t < ST - 1 else f"used{slot}"), 1)
                wait_evacuated(pe, "uq", 5, layer=layer)
                for t in range(2):
                    pe.wait_ge(sem("roped"), 3 * layer + t + 1)
                    nc.tensor.matmul(ps[:, 5, :], swap, qr[:, t, :], start=True, stop=True)\
                        .then_inc(sem("swapped"), 1)

                pe.wait_ge(sem("roped"), 3 * layer + 3)

                def operands(m, i):
                    kind, hd, c = MAPS[m]
                    qs = slice(i * P, (i + 1) * P)
                    if kind == "A":
                        r = slice(64 * (hd % 2), 64 * (hd % 2) + 64)
                        return [(proj[r, QA_IN + hd // 2, qs], proj[r, KA_IN + hd // 2, :])]
                    if kind == "C":
                        r = slice(64 * (hd % 2) + 32 * c, 64 * (hd % 2) + 32 * c + 32)
                        return [(proj[r, QC_IN + hd // 2, qs], proj[r, KC_IN + hd // 2, :])]
                    r = slice(64 * (hd % 2), 64 * (hd % 2) + 64)
                    e = slice(32 * (hd % 4), 32 * (hd % 4) + 32)
                    return [(qb[r, hd // 2, qs], kb[r, hd // 2, :]),
                            (qr[e, hd // 4, qs], proj[e, PE_IN, :])]

                def scores(m):
                    for i in range(ST):
                        if m == 0:
                            if i == 0:
                                for t in range(ST):
                                    wait_evacuated(pe, "uv", t, layer=layer)
                        elif MAPS[m - 1][0] == "B":
                            pe.wait_ge(sem("exps"), (layer * len(MAPS) + m - 1) * ST + i + 1)
                        else:
                            pe.wait_ge(sem("scores_read"), (layer * len(DVE_READ) + DVE_READ.index(m - 1)) * ST + i + 1)
                        pairs = operands(m, i)
                        for n, (a, b) in enumerate(pairs):
                            mm = nc.tensor.matmul(ps[:, i, :], a, b, start=(n == 0), stop=(n == len(pairs) - 1))
                        mm.then_inc(sem("scores"), 1)

                def values(m):
                    kind, hd, _ = MAPS[m]
                    if kind == "A":
                        return v_ac, 64 * hd
                    if kind == "C":
                        return v_ac, 256 + 64 * hd
                    return v_b, 64 * hd

                def output(m):
                    o = OUTPUTS.index(m)
                    src, at = values(m)
                    pe.wait_ge(sem("probs_ready"), layer * len(OUTPUTS) + o + 1)

                    def weigh(kt):
                        pe.wait_ge(sem("probs_t"), (layer * len(OUTPUTS) + o) * ST + kt + 1)
                        lo = 64 * (o % 2)
                        nc.tensor.matmul(ps[lo:lo + 64, 6 + o // 2 % 2, :], src[:, kt, at:at + 64], probs_t[:, kt, :],
                                         start=(kt == 0), stop=(kt == ST - 1)).then_inc(sem("weighed"), 1)

                    if o >= 4 and o % 2 == 0:
                        pe.wait_ge(sem("mixed"), 8 * layer + o // 2 - 1)
                    for kt in range(ST):
                        if o or kt > 1:
                            pe.wait_ge(sem("probs_t"), (layer * len(OUTPUTS) + o) * ST + kt - 1)
                        for i in range(ST):
                            mm = nc.tensor.transpose(ps[:, 4 + kt % 2, i * P:(i + 1) * P],
                                                     probs[m % 3][:, i, kt * P:(kt + 1) * P], ident)
                        mm.then_inc(sem("turned"), 1)
                        if kt:
                            weigh(kt - 1)
                    weigh(ST - 1)

                for what, m in PE_ORDER:
                    (scores if what == "scores" else output)(m)
                for t in range(2):
                    pe.wait_ge(sem("head_sq"), 2 * layer + t + 1)
                    nc.tensor.matmul(ps[:, 4 + t, :], consts[:, HEAD_ONES, :], tmp2[:, t, :], start=True, stop=True)\
                        .then_inc(sem("head_sum"), 1)
                pe.wait_ge(sem("heads_normed"), 2 * layer + 2)
                pe_product(pe, "out2", lambda k: mixed[:, k, :], layer)
                n, q = norm_at(7, layer)
                ffn("up_b", "down_b", "xn_b", n, q + 8, layer)
            pe_norm(pe, N_LAST, 24 + SQ_PER_LAYER * LAYERS + 8)

        @block.scalar
        def _(act):
            act.wait_ge(sem("in_cols"), 16)
            nc.scalar.activation(cact, cols[:, COL1["c"]:COL1["c"] + DT], ACT.Silu).then_inc(sem("cact"), 1)
            act.wait_ge(sem("lam_dots"), 2 * LAYERS)
            nc.scalar.activation(lam_s[:, :], lam_s[:, :], ACT.Exp).then_inc(sem("lam_exp"), 1)
            act.wait_ge(sem("in_x"), 16)
            for t in range(DT):
                act_square(act, t, tmp[:, t % 2, :], h[:, t, :])
            act_norm(act, 0)
            for k in range(DT):
                act.wait_ge(sem("scaled1"), k + 1)
                nc.scalar.activation(xn[:, k, :], xn[:, k, :], ACT.Identity, bias=mod[:, k:k + 1])\
                    .then_inc(sem("xn1"), 1)
            for half in range(2):
                for st in range(ST):
                    t = ST * half + st
                    wait_token_tile(act, "v", half, st)
                    nc.scalar.activation(v_tok[:, st, half * S:(half + 1) * S], bank_ap("v", t), ACT.Gelu_apprx_tanh)\
                        .then_inc(evacuated("v", t), 1)
            for t in range(8):
                wait_tile(act, "u", t)
                nc.scalar.activation(gu[:, t, :], bank_ap("u", t), ACT.Gelu_apprx_tanh)\
                    .then_inc(evacuated("u", t), 1)
            act.wait_ge(sem("v_var"), 1)
            nc.scalar.activation(nrm[:, 2, :], nrm[:, 1, :], ACT.Sqrt).then_inc(sem("v_root"), 1)
            act.wait_ge(sem("f_abs"), 1)
            nc.scalar.activation(rows[:, 2, :], rows[:, 2, :], ACT.Exp, scale=-1.0)
            act.drain()
            nc.scalar.activation(rows[:, 2, :], rows[:, 2, :], ACT.Ln, bias=1.0).then_inc(sem("f_log"), 1)
            act.wait_ge(sem("m_rows"), 1)
            nc.scalar.activation(rows[:, 5, :], rows[:, 5, :], ACT.Exp, scale=-1.0).then_inc(sem("rows_ready"), 1)
            for t in range(8):
                wait_tile(act, "ga", t)
                wait(act, "ga_used", t - 3)
                nc.scalar.activation(tmp[:, t % 4, :], bank_ap("ga", t), ACT.Sigmoid)\
                    .then_inc(evacuated("ga", t), 1)
            for n in range(2 * HEADS):
                act.wait_ge(sem("spread"), n + 1)
                dst = (neg_m, e_mt)[n % 2]
                nc.scalar.activation(dst[:, n // 2, :], ps[:, 4 + n % 2, :], ACT.Copy).then_inc(sem("spread_read"), 1)
            for t in range(16):
                wait_evacuated(act, "qk", t)
                dst = qf[:, t, :] if t < 8 else kf[:, t - 8, :]
                nc.scalar.activation(dst, tmp[:, t % 4, :], ACT.Silu).then_inc(sem("qk_silu"), 1)
            for half in range(2):
                for st in range(ST):
                    t = ST * half + st
                    wait_token_tile(act, "mv", half, st)
                    nc.scalar.activation(mv[:, st, half * S:(half + 1) * S], bank_ap("mv", t), ACT.Copy)\
                        .then_inc(evacuated("mv", t), 1)
            for t in range(8):
                wait_tile(act, "o", t)
                nc.scalar.activation(so[:, t, :], bank_ap("o", t), ACT.Sigmoid).then_inc(evacuated("o", t), 1)
            for t in range(8):
                wait_tile(act, "gb", t)
                wait(act, "gb_used", t - 3)
                nc.scalar.activation(tmp[:, t % 4, :], bank_ap("gb", t), ACT.Sigmoid)\
                    .then_inc(evacuated("gb", t), 1)

            def cell_exp(hd):
                for j in range(ST):
                    act.wait_ge(sem("cell_arg"), ST * hd + j + 1)
                    w = cell_w[:, j, 0:S - j * P]
                    nc.scalar.activation(w, w, ACT.Exp).then_inc(sem("cell_exp"), 1)

            cell_exp(0)
            for hd in range(HEADS):
                if hd + 1 < HEADS:
                    cell_exp(hd + 1)
                for v in range(VT):
                    act.wait_ge(sem("cell_centred"), VT * hd + v + 1)
                    nc.scalar.activation(tmp[:, v, :], qf[:, VT * hd + v, :], ACT.Square).then_inc(sem("cell_sq"), 1)
            for hd in range(HEADS):
                act.wait_ge(sem("cell_recip"), hd + 1)
                nc.scalar.activation(e_mt[:, hd, :], e_mt[:, hd, :], ACT.Sqrt).then_inc(sem("cell_root"), 1)
            for t in range(DT):
                wait_evacuated(act, "out1", t)
                act_square(act, SQUARES[1] + t, tmp[:, t % 2, :], h[:, t, :])
            act_norm(act, 1)
            for k in range(DT):
                act.wait_ge(sem("scaled2"), k + 1)
                nc.scalar.activation(xn[:, k, :], xn[:, k, :], ACT.Identity, bias=mod[:, 24 + k:25 + k])\
                    .then_inc(sem("xn2"), 1)

            def ff1(it, places):
                for u in places:
                    wait_tile(act, "ff1", u, it)
                    wait(act, f"ff1_squared{u % 4}", it * 2 + u // 4)
                    nc.scalar.activation(tmp[:, u % 4, :], bank_ap("ff1", u), ACT.Relu)\
                        .then_inc(evacuated("ff1", u), 1)

            steps(nc.scalar, 32, 8, ff1, peel=1)

            def ff2(it, places):
                for u in places:
                    wait_evacuated(act, "ff2", u, it, 4)
                    act_square(act, SQUARES[2] + it * 4 + u, tmp[:, u % 2, :], h[:, it * 4 + u, :])

            steps(nc.scalar, 8, 4, ff2)
            act_norm(act, 2)
            for t in range(DT):
                act.wait_ge(sem("block1"), t + 1)
                act_square(act, 24 + t, tmp2[:, t % 2, :], h[:, t, :])
            for n in range(2):
                act.wait_ge(sem("angles"), n + 1)
                tab = (cos_t, sin_t)[n]
                nc.scalar.activation(tab, tab, ACT.Sin).then_inc(sem("sines"), 1)

            def ffn(name, down, base_q, layer):
                def up(it, places):
                    for u in places:
                        if u % 2:
                            continue
                        wait_tile(act, name, u, it, layer)
                        f = u // 2
                        b, before = bank(name, u + 1, it, 8, layer)
                        act.wait_ge(sem(f"evacuated{b}"), before - 1)
                        nc.scalar.activation(tmp2[:, f, :], bank_ap(name, u), ACT.Silu)\
                            .then_inc(evacuated(name, u), 1)

                steps(nc.scalar, 44, 8, up)

                def dn(it, places):
                    for u in places:
                        wait_evacuated(act, down, u, it, 4, layer)
                        act_square(act, base_q + it * 4 + u, tmp2[:, SQ_FIRST[down] + (u + SQ_OFF[down]) % 2, :],
                                   h[:, it * 4 + u, :])

                steps(nc.scalar, 8, 4, dn)

            with nc.scalar.Fori(0, LAYERS) as layer:
                act_norm(act, norm_at(3, layer)[0])
                ffn("up_a", "down_a", norm_at(4, layer)[1], layer)
                act_norm(act, norm_at(4, layer)[0])
                for t in range(1, 14, 2):
                    wait_tile(act, "in", t, 0, layer)
                    nc.scalar.activation(proj[:, t, :], bank_ap("in", t), ACT.Copy).then_inc(evacuated("in", t), 1)
                for t in range(ST):
                    wait_token_tile(act, "in_v", 0, t, layer, 1)
                    nc.scalar.activation(v_ac[:, t, :], bank_ap("in_v", t), ACT.Copy)\
                        .then_inc(evacuated("in_v", t), 1)
                wait_evacuated(act, "in", 12, layer=layer)
                for j, first, count in ((5, Q_IN, Q_TILES), (6, KV_IN, KV_TILES)):
                    n, q = norm_at(j, layer)
                    for t in range(count):
                        act_square(act, q + t, tmp2[:, sq_parity(j, t), :], proj[:, first + t, :])
                    act_norm(act, n)
                for t in range(6):
                    wait_tile(act, "uq", t, 0, layer)
                    dst = qb[:, t, :] if t < 4 else qr[:, t - 4, :]
                    nc.scalar.activation(dst, bank_ap("uq", t), ACT.Copy).then_inc(evacuated("uq", t), 1)
                for t in range(4):
                    act.wait_ge(sem("uk_tile"), 4 * layer + t + 1)
                    nc.scalar.activation(kb[:, t, :], bank_ap("uk", t), ACT.Copy).then_inc(evacuated("uk", t), 1)
                for t in range(ST):
                    if t < ST - 1:
                        act.wait_ge(sem("uv_tile"), 3 * layer + t + 1)
                    else:
                        slot, before = chunk("ukv", 0, 0, 0, layer)
                        act.wait_ge(sem(f"used{slot}"), before + 1)
                    nc.scalar.activation(v_b[:, t, :], bank_ap("uv", t), ACT.Copy).then_inc(evacuated("uv", t), 1)

                def scores(m):
                    kind = MAPS[m][0]
                    scale = {"A": SCALE_A, "B": SCALE_B, "C": SCALE_C}[kind]
                    if kind == "B" and m >= 3:
                        o = OUTPUTS.index(m - 3)
                        act.wait_ge(sem("turned"), (layer * len(OUTPUTS) + o) * ST + ST)
                    for i in range(ST):
                        act.wait_ge(sem("maxima"), (layer * len(MAPS) + m) * ST + i + 1)
                        dst = probs[m % 3][:, i, :]
                        src = ps[:, i, :] if kind == "B" else dst
                        nc.scalar.activation(dst, src, ACT.Exp, bias=soft[:, m % 3, neg_mx, i:i + 1], scale=scale,
                                             accum_out=soft[:, m % 3, rsum, i:i + 1]).then_inc(sem("exps"), 1)

                def output(m):
                    o = OUTPUTS.index(m)
                    for kt in range(ST):
                        act.wait_ge(sem("turned"), (layer * len(OUTPUTS) + o) * ST + kt + 1)
                        if o:
                            act.wait_ge(sem("weighed"), (layer * len(OUTPUTS) + o - 1) * ST + kt + 1)
                        nc.scalar.activation(probs_t[:, kt, :], ps[:, 4 + kt % 2, :], ACT.Copy)\
                            .then_inc(sem("probs_t"), 1)

                for what, m in SOFT_ORDER:
                    (scores if what == "scores" else output)(m)
                for t in range(2):
                    act.wait_ge(sem("mixed"), 8 * layer + 7 + t)
                    nc.scalar.activation(tmp2[:, t, :], mixed[:, 6 + t, :], ACT.Square).then_inc(sem("head_sq"), 1)
                for t in range(2):
                    act.wait_ge(sem("head_recip"), 2 * layer + t + 1)
                    nc.scalar.activation(tmp2[:, t, :], tmp2[:, t, :], ACT.Sqrt).then_inc(sem("head_root"), 1)
                n, q = norm_at(7, layer)
                for t in range(DT):
                    wait_evacuated(act, "out2", t, layer=layer)
                    act_square(act, q + t, tmp2[:, sq_parity(7, t), :], h[:, t, :])
                act_norm(act, n)
                ffn("up_b", "down_b", norm_at(3, layer + 1)[1], layer)
            act_norm(act, N_LAST)

        @block.vector
        def _(dve):
            nc.vector.memset(ssq[:, :], 0.0)
            dve.wait_ge(sem("in_lam"), 16)
            dve.wait_ge(sem("in_cols"), 16)
            dve.wait_ge(sem("in_consts"), 16)
            for layer in range(LAYERS):
                for n in range(2):
                    nc.vector.tensor_tensor(lam_w[:, :], lam_in[:, layer, 2 * n, :], lam_in[:, layer, 2 * n + 1, :],
                                            ALU.mult)
                    dve.drain()
                    nc.vector.tensor_reduce(lam_s[:, 2 * layer + n:2 * layer + n + 1], lam_w[:, :], AX_X, ALU.add)\
                        .then_inc(sem("lam_dots"), 1)
                    dve.drain()
            dve.wait_ge(sem("lam_exp"), 1)
            for layer in range(LAYERS):
                at = N_COLS_1 + layer * N_COLS_2
                neg, head = at + COL2["neg_lam"], at + COL2["head"]
                nc.vector.tensor_scalar(cols[:, neg:neg + 1], lam_s[:, 2 * layer + 1:2 * layer + 2],
                                        -LAMBDA_INIT[layer], None, ALU.add)
                dve.drain()
                nc.vector.tensor_tensor(cols[:, neg:neg + 1], cols[:, neg:neg + 1], lam_s[:, 2 * layer:2 * layer + 1],
                                        ALU.subtract)
                nc.vector.tensor_scalar(cols[:, head:head + 1], cols[:, head:head + 1], 1.0 - LAMBDA_INIT[layer],
                                        None, ALU.mult)
            for t in range(DT):
                dve_add_square(dve, t, tmp[:, t % 2, :])

            def ada(it, places):
                for c in places:
                    slot, before = chunk("ada", c, it, 4, 0)
                    dve.wait_ge(sem(f"used{slot}"), before + 1)
                    at = it * 8 + 2 * c
                    nc.vector.tensor_tensor(mod[:, bass.ds(at, 2)], bank_ap("ada", c)[:, 0:2],
                                            cols[:, bass.ds(COL1["b_ada"] + at, 2)], ALU.add)\
                        .then_inc(evacuated("ada", c), 1)

            steps(nc.vector, 24, 4, ada)
            dve.drain()
            for gain, base, g in ((gain1, 8, COL1["norm1"]), (gain2, 32, COL1["norm2"])):
                nc.vector.scalar_tensor_tensor(gain, mod[:, base:base + 8], 1.0, cols[:, g:g + 8], ALU.add, ALU.mult)
            dve.drain()
            dve_norm(dve, 0, D)
            for k in range(DT):
                scaled(dve, xn[:, k, :], h[:, k, :], gain1[:, k:k + 1], "scaled1")

            dve.wait_ge(sem("gates_made"), 1)
            dve.wait_ge(sem("in_gates"), 32)
            nc.vector.tensor_scalar(rows[:, 0, :], ps[0:4, 5, :], gate_b[:, 0:1], None, ALU.add)
            nc.vector.tensor_scalar(rows[:, 1, :], ps[32:36, 5, :], gate_b[:, 1:2], None, ALU.add)
            dve.drain()
            nc.vector.scalar_tensor_tensor(rows[:, 2, :], rows[:, 1, :], -1.0, rows[:, 1, :], ALU.mult, ALU.max)\
                .then_inc(sem("f_abs"), 1)

            for st in range(ST):
                for half in range(2):
                    wait_evacuated(dve, "v", ST * half + st)
                    nc.vector.bn_stats(bn[:, st, half, :], v_tok[:, st, half * S:(half + 1) * S])
                dve.drain()
                nc.vector.bn_aggr(bn_mv[:, st, :], bn[:, st, :, :])
            dve.drain()
            nc.vector.tensor_scalar(nrm[:, 0, :], bn_mv[:, :, 1], EPS, None, ALU.add)
            dve.drain()
            nc.vector.reciprocal(nrm[:, 1, :], nrm[:, 0, :]).then_inc(sem("v_var"), 1)
            dve.wait_ge(sem("v_root"), 1)
            for st in range(ST):
                nc.vector.tensor_scalar(v_tok[:, st, :], v_tok[:, st, :], bn_mv[:, st, 0:1], nrm[:, 2, st:st + 1],
                                        ALU.subtract, ALU.mult).then_inc(sem("v_normed"), 1)

            dve.wait_ge(sem("f_log"), 1)
            nc.vector.scalar_tensor_tensor(rows[:, 1, :], rows[:, 1, :], 0.0, rows[:, 2, :], ALU.min, ALU.subtract)
            nc.vector.memset(rows[:, 7, :], 1.0)
            dve.drain()
            nc.vector.tensor_tensor_scan(rows[:, 3, :], rows[:, 7, :], rows[:, 1, :], 0.0, ALU.mult, ALU.add)
            dve.drain()
            nc.vector.tensor_tensor(rows[:, 2, :], rows[:, 0, :], rows[:, 3, :], ALU.subtract)
            dve.drain()
            nc.vector.tensor_tensor_scan(rows[:, 6, :], rows[:, 7, :], rows[:, 2, :], 0.0, ALU.mult, ALU.max)
            dve.drain()
            nc.vector.tensor_scalar(rows[:, 4, :], rows[:, 6, :], -1.0, None, ALU.mult)
            nc.vector.tensor_tensor(rows[:, 5, :], rows[:, 3, :], rows[:, 6, :], ALU.add).then_inc(sem("m_rows"), 1)

            for g in range(GROUPS):
                dve.wait_ge(sem("ws_sums"), g // 4 + 1)
                nc.vector.scalar_tensor_tensor(mix_base[:, g, :], ps[:, 4, (g % 4) * P:(g % 4 + 1) * P],
                                               cols[:, COL1["ln_b"] + g:COL1["ln_b"] + g + 1], bs_row[:, g, :],
                                               ALU.mult, ALU.add).then_inc(sem("ws_base"), 1)
            dve.drain()
            for g in range(GROUPS):
                dve.wait_ge(sem("mix_tile"), g + 1)
                base = mix_base[:, g:g + 1, :].to_broadcast([P, ST, P])
                nc.vector.scalar_tensor_tensor(merged[:, g, :].rearrange("p (b t) -> p b t", b=ST),
                                               bank_ap("mix", g).rearrange("p (b t) -> p b t", b=ST),
                                               cols[:, COL1["ln_g"] + g:COL1["ln_g"] + g + 1], base,
                                               ALU.mult, ALU.add).then_inc(evacuated("mix", g), 1)
                wait_evacuated(dve, "u", g)
                dve.drain()
                nc.vector.tensor_tensor(merged[:, g, :], merged[:, g, :], gu[:, g, :], ALU.mult)
            dve.drain()
            for t in range(8):
                wait_evacuated(dve, "ga", t)
                nc.vector.tensor_tensor(merged[:, t, :], merged[:, t, :], tmp[:, t % 4, :], ALU.mult)\
                    .then_inc(sem("ga_used"), 1)
            dve.drain()
            for t in range(16):
                wait_tile(dve, "qk", t % 8, t // 8)
                wait(dve, "qk_silu", t - 3)
                acc, src = tmp[:, t % 4, :], bank_ap("qk", t % 8)

                def tap(j, t=t):
                    return cols[:, COL1["conv_w"] + 16 * j + t:COL1["conv_w"] + 16 * j + t + 1]

                nc.vector.tensor_scalar(acc, src, tap(CONV_K - 1), cols[:, COL1["conv_b"] + t:COL1["conv_b"] + t + 1],
                                        ALU.mult, ALU.add)
                for back in range(1, CONV_K):
                    dve.drain()
                    last = nc.vector.scalar_tensor_tensor(acc[:, back:S], src[:, 0:S - back], tap(CONV_K - 1 - back),
                                                          acc[:, back:S], ALU.mult, ALU.add)
                last.then_inc(evacuated("qk", t % 8), 1)
            dve.wait_ge(sem("a_cols"), 1)
            nc.vector.tensor_copy(stat[:, 24:40], ps[:, 7, 0:ST * HEADS])
            dve.drain()
            for t in range(8):
                wait_evacuated(dve, "gb", t)
                wait_evacuated(dve, "o", t)
                nc.vector.tensor_tensor(so[:, t, :], so[:, t, :], tmp[:, t % 4, :], ALU.mult)\
                    .then_inc(sem("gb_used"), 1)
            dve.wait_ge(sem("spread_read"), 2 * HEADS)

            def cell_args(hd):
                for j in range(ST):
                    nc.vector.tensor_scalar(cell_w[:, j, 0:S - j * P], neg_m[:, hd, j * P:S], a_col[:, j, hd:hd + 1],
                                            0.0, ALU.add, ALU.min).then_inc(sem("cell_arg"), 1)

            def cell_weights(hd):
                wait(dve, "cell_sums", hd)
                for j in range(ST):
                    t = ST * hd + j
                    dve.wait_ge(sem("cell_tile"), t + 1)
                    dve.wait_ge(sem("cell_masked"), t + 1)
                    nc.vector.scalar_tensor_tensor(cell_s[:, j, 0:S - j * P], bank_ap("cell", t)[:, 0:S - j * P],
                                                   HEAD_DIM**-0.5, cell_w[:, j, 0:S - j * P], ALU.mult, ALU.mult)\
                        .then_inc(evacuated("cell", t), 1)

            def cell_out(hd):
                dve.wait_ge(sem("cell_sums"), hd + 1)
                nc.vector.tensor_copy(tmp[:, 2, :], ps[:, 6, :])
                dve.drain()
                nc.vector.scalar_tensor_tensor(tmp[:, 3, :], tmp[:, 2, :], -1.0, tmp[:, 2, :], ALU.mult, ALU.max)
                dve.drain()
                nc.vector.tensor_tensor(tmp[:, 2, :], tmp[:, 3, :], e_mt[:, hd, :], ALU.max)
                dve.drain()
                nc.vector.reciprocal(tmp[:, 3, :], tmp[:, 2, :])
                dve.drain()
                for v in range(VT):
                    nc.vector.tensor_tensor(qf[:, VT * hd + v, :], ps[:, 4 + v, :], tmp[:, 3, :], ALU.mult)\
                        .then_inc(sem("cell_h"), 1)
                dve.wait_ge(sem("cell_mean"), hd + 1)
                for v in range(VT):
                    nc.vector.tensor_tensor(qf[:, VT * hd + v, :], qf[:, VT * hd + v, :], ps[:, 7, :], ALU.subtract)\
                        .then_inc(sem("cell_centred"), 1)
                dve.wait_ge(sem("cell_var"), hd + 1)
                nc.vector.tensor_scalar(tmp[:, 2, :], ps[:, 7, :], EPS, None, ALU.add)\
                    .then_inc(sem("cell_var_read"), 1)
                dve.drain()
                nc.vector.reciprocal(e_mt[:, hd, :], tmp[:, 2, :]).then_inc(sem("cell_recip"), 1)
                dve.drain()

            cell_args(0)
            cell_weights(0)
            for hd in range(HEADS):
                if hd + 1 < HEADS:
                    dve.drain()
                    cell_args(hd + 1)
                    cell_weights(hd + 1)
                cell_out(hd)
            for hd in range(HEADS):
                dve.wait_ge(sem("cell_root"), hd + 1)
                for v in range(VT):
                    t = VT * hd + v
                    nc.vector.scalar_tensor_tensor(qf[:, t, :], qf[:, t, :],
                                                   cols[:, COL1["hn_g"] + t:COL1["hn_g"] + t + 1], e_mt[:, hd, :],
                                                   ALU.mult, ALU.mult)
                dve.drain()
                for t in (VT * hd, VT * hd + 1):
                    nc.vector.tensor_tensor(qf[:, t, :], qf[:, t, :], so[:, t, :], ALU.mult)
                dve.drain()
                for t in (VT * hd, VT * hd + 1):
                    nc.vector.tensor_tensor(merged[:, t, :], merged[:, t, :], qf[:, t, :], ALU.add)\
                        .then_inc(sem("merged_ready"), 1)
            for t in range(8):
                wait_tile(dve, "out1", t)
                nc.vector.scalar_tensor_tensor(h[:, t, :], bank_ap("out1", t), mod[:, 16 + t:17 + t], h[:, t, :],
                                               ALU.mult, ALU.add).then_inc(evacuated("out1", t), 1)
                dve_add_square(dve, SQUARES[1] + t, tmp[:, t % 2, :])
            dve_norm(dve, 1, D)
            for k in range(DT):
                scaled(dve, xn[:, k, :], h[:, k, :], gain2[:, k:k + 1], "scaled2")

            def ff1(it, places):
                for u in places:
                    wait_evacuated(dve, "ff1", u, it, 8)
                    nc.vector.tensor_tensor(hid1[:, it * 8 + u, :], tmp[:, u % 4, :], tmp[:, u % 4, :], ALU.mult)\
                        .then_inc(sem(f"ff1_squared{u % 4}"), 1)

            steps(nc.vector, 32, 8, ff1)

            def ff2(it, places):
                for u in places:
                    wait_tile(dve, "ff2", u, it)
                    t = it * 4 + u
                    nc.vector.scalar_tensor_tensor(h[:, t, :], bank_ap("ff2", u), mod[:, bass.ds(40 + t, 1)],
                                                   h[:, t, :], ALU.mult, ALU.add)\
                        .then_inc(evacuated("ff2", u), 1)
                    dve_add_square(dve, SQUARES[2] + t, tmp[:, u % 2, :])

            steps(nc.vector, 8, 4, ff2)
            dve_norm(dve, 2, D)
            for t in range(DT):
                scaled(dve, h[:, t, :], h[:, t, :], cols[:, COL1["final1"] + t:COL1["final1"] + t + 1], "block1")
            for t in range(DT):
                dve_add_square(dve, 24 + t, tmp2[:, t % 2, :])

            dve.wait_ge(sem("in_pos"), 16)
            pos_c = stat[:, 40:44]
            pos_r, turns = tmp2[:, 2, :], tmp2[:, 3, :]
            nc.vector.tensor_copy(pos_r, pos_i[:, 0:S])
            nc.vector.tensor_copy(pos_c, pos_i[:, S:S + ST])
            dve.drain()
            for i in range(ST):
                nc.vector.tensor_scalar(turns, pos_r, pos_c[:, i:i + 1], None, ALU.subtract)
                dve.drain()
                nc.vector.scalar_tensor_tensor(dist[:, i, :], turns, -1.0, turns, ALU.mult, ALU.max)
                dve.drain()
            nc.vector.tensor_scalar(pos_r, pos_r, cols[:, COL1["inv_freq"]:COL1["inv_freq"] + 1], None, ALU.mult)
            dve.drain()
            ROUND = 12582912.0
            HIGH = 6.28125
            LOW = TWO_PI - HIGH
            for tab, quarter in ((cos_t, 0.25), (sin_t, 0.0)):
                nc.vector.tensor_scalar(turns, pos_r, 1.0 / TWO_PI, quarter, ALU.mult, ALU.add)
                dve.drain()
                nc.vector.tensor_scalar(turns, turns, ROUND, ROUND, ALU.add, ALU.subtract)
                dve.drain()
                nc.vector.scalar_tensor_tensor(tab, turns, -HIGH, pos_r, ALU.mult, ALU.add)
                dve.drain()
                nc.vector.scalar_tensor_tensor(tab, turns, -LOW, tab, ALU.mult, ALU.add)
                dve.drain()
                nc.vector.tensor_scalar(tab, tab, quarter * TWO_PI, 3.1415925, ALU.add, ALU.min)
                dve.drain()
                nc.vector.tensor_scalar(tab, tab, -3.1415925, None, ALU.max).then_inc(sem("angles"), 1)
            dve.wait_ge(sem("sines"), 2)
            nc.vector.tensor_scalar(sin_t, sin_t, cols[:, COL1["sin_sign"]:COL1["sin_sign"] + 1], None, ALU.mult)
            dve.drain()

            def col(name, n=0):
                return lcols[:, COL2[name] + n:COL2[name] + n + 1]

            def ffn(name, down, normed, gain, n, base_q, layer):
                dve_norm(dve, n, D)
                for k in range(DT):
                    scaled(dve, xn[:, k, :], h[:, k, :], col(gain, k), normed)

                def up(it, places):
                    for u in places:
                        if u % 2 == 0:
                            continue
                        f = u // 2
                        wait_evacuated(dve, name, u - 1, it, 8, layer)
                        wait_tile(dve, name, u, it, layer)
                        nc.vector.tensor_tensor(hid2[:, it * 4 + f, :], bank_ap(name, u), tmp2[:, f, :], ALU.mult)\
                            .then_inc(evacuated(name, u), 1)

                steps(nc.vector, 44, 8, up)
                def dn(it, places):
                    for u in places:
                        wait_tile(dve, down, u, it, layer)
                        nc.vector.scalar_tensor_tensor(h[:, it * 4 + u, :], bank_ap(down, u), 0.5,
                                                       h[:, it * 4 + u, :], ALU.mult, ALU.add)\
                            .then_inc(evacuated(down, u), 1)
                        dve_add_square(dve, base_q + it * 4 + u,
                                       tmp2[:, SQ_FIRST[down] + (u + SQ_OFF[down]) % 2, :])

                steps(nc.vector, 8, 4, dn)

            with nc.vector.Fori(0, LAYERS) as layer:
                dve.drain()
                nc.vector.tensor_copy(lcols[:, :], cols[:, bass.ds(N_COLS_1 + layer * N_COLS_2, N_COLS_2)])
                dve.drain()
                ffn("up_a", "down_a", "xn_a", "ffn_a", norm_at(3, layer)[0], norm_at(4, layer)[1], layer)
                dve_norm(dve, norm_at(4, layer)[0], D)
                for k in range(DT):
                    scaled(dve, xn[:, k, :], h[:, k, :], col("mix", k), "xn_m")
                for t in range(0, 14, 2):
                    wait_tile(dve, "in", t, 0, layer)
                    nc.vector.tensor_copy(proj[:, t, :], bank_ap("in", t)).then_inc(evacuated("in", t), 1)

                def rope(dst, count):
                    dve.wait_ge(sem("swapped"), count)
                    nc.vector.tensor_tensor(tmp2[:, 2, :], ps[:, 5, :], sin_t, ALU.mult)
                    nc.vector.tensor_tensor(dst, dst, cos_t, ALU.mult)
                    dve.drain()
                    nc.vector.tensor_tensor(dst, dst, tmp2[:, 2, :], ALU.add).then_inc(sem("roped"), 1)

                rope(proj[:, PE_IN, :], 3 * layer + 1)
                for j, first, count, gain, name, width in (
                        (5, Q_IN, Q_TILES, "qn", "q_normed", Q_TILES * P),
                        (6, KV_IN, KV_TILES, "kvn", "kv_normed", KV_TILES * P)):
                    n, q = norm_at(j, layer)
                    for t in range(count):
                        dve_add_square(dve, q + t, tmp2[:, sq_parity(j, t), :])
                    dve_norm(dve, n, width)
                    for t in range(count):
                        scaled(dve, proj[:, first + t, :], proj[:, first + t, :], col(gain, t), name)
                for t in range(2):
                    rope(qr[:, t, :], 3 * layer + 2 + t)

                def scores(m):
                    kind, hd, c = MAPS[m]
                    scale = {"A": SCALE_A, "B": SCALE_B, "C": SCALE_C}[kind]
                    st = soft[:, m % 3, :, :]
                    if kind == "A":
                        dve.drain()
                        dve.wait_ge(sem("in_log_c"), 16)
                        if hd == 0:
                            wait_evacuated(dve, "uv", ST - 1, layer=layer)
                        for i in range(ST):
                            nc.vector.scalar_tensor_tensor(bias_a[:, i, :], dist[:, i, :],
                                                           -SLOPES[2 * hd] / SCALE_A, log_c[:, i, :],
                                                           ALU.mult, ALU.add)
                        dve.drain()
                    if kind != "B" and m >= 3 and m - 3 in OUTPUTS:
                        o = OUTPUTS.index(m - 3)
                        dve.wait_ge(sem("turned"), (layer * len(OUTPUTS) + o) * ST + ST)
                    for i in range(ST):
                        dve.wait_ge(sem("scores"), (layer * len(MAPS) + m) * ST + i + 1)
                        dst = probs[m % 3][:, i, :]
                        if kind == "A":
                            nc.vector.tensor_tensor(dst, ps[:, i, :], bias_a[:, i, :], ALU.add)\
                                .then_inc(sem("scores_read"), 1)
                        elif kind == "C":
                            nc.vector.scalar_tensor_tensor(dst, dist[:, i, :], -SLOPES[2 * hd + 1] / SCALE_C,
                                                           ps[:, i, :], ALU.mult, ALU.add)\
                                .then_inc(sem("scores_read"), 1)
                        if kind != "B":
                            dve.drain()
                        nc.vector.tensor_reduce(st[:, mx, i:i + 1], ps[:, i, :] if kind == "B" else dst, AX_X, ALU.max)
                        dve.drain()
                        nc.vector.tensor_scalar(st[:, neg_mx, i:i + 1], st[:, mx, i:i + 1], -scale, None, ALU.mult)\
                            .then_inc(sem("maxima"), 1)

                def output(m):
                    kind, hd, c = MAPS[m]
                    o = OUTPUTS.index(m)
                    st = soft[:, m % 3, :, :]
                    dve.wait_ge(sem("exps"), (layer * len(MAPS) + m) * ST + ST)
                    nc.vector.reciprocal(st[:, rinv, :], st[:, rsum, :])
                    if kind == "C":
                        other = soft[:, (m - 1) % 3, :, :]
                        nc.vector.reciprocal(other[:, rinv, :], other[:, rsum, :])
                        dve.drain()
                        nc.vector.tensor_scalar(st[:, rinv, :], st[:, rinv, :], col("neg_lam"), None, ALU.mult)
                        for i in range(ST):
                            nc.vector.tensor_scalar(probs[(m - 1) % 3][:, i, :], probs[(m - 1) % 3][:, i, :],
                                                    other[:, rinv, i:i + 1], None, ALU.mult)
                    dve.drain()
                    for i in range(ST):
                        p = probs[m % 3][:, i, :]
                        if kind == "C":
                            last = nc.vector.scalar_tensor_tensor(p, p, st[:, rinv, i:i + 1],
                                                                  probs[(m - 1) % 3][:, i, :], ALU.mult, ALU.add)
                        else:
                            last = nc.vector.tensor_scalar(p, p, st[:, rinv, i:i + 1], None, ALU.mult)
                    last.then_inc(sem("probs_ready"), 1)
                    dve.drain()
                    if o and o % 2 == 0:
                        take_pair(o // 2 - 1)

                def take_pair(pair):
                    dve.wait_ge(sem("weighed"), (layer * len(OUTPUTS) + 2 * pair + 2) * ST)
                    nc.vector.tensor_copy(mixed[:, pair, :], ps[:, 6 + pair % 2, :]).then_inc(sem("mixed"), 1)

                for what, m in SOFT_ORDER:
                    (scores if what == "scores" else output)(m)
                take_pair(7)
                for t in range(2):
                    dve.wait_ge(sem("head_sum"), 2 * layer + t + 1)
                    nc.vector.tensor_scalar(tmp2[:, 2 + t, :], ps[:, 4 + t, :], 1.0 / 64, EPS, ALU.mult, ALU.add)
                    dve.drain()
                    nc.vector.reciprocal(tmp2[:, t, :], tmp2[:, 2 + t, :]).then_inc(sem("head_recip"), 1)
                for t in range(2):
                    dve.wait_ge(sem("head_root"), 2 * layer + t + 1)
                    nc.vector.scalar_tensor_tensor(mixed[:, 6 + t, :], mixed[:, 6 + t, :], col("head"),
                                                   tmp2[:, t, :], ALU.mult, ALU.mult)\
                        .then_inc(sem("heads_normed"), 1)
                n, q = norm_at(7, layer)
                for t in range(DT):
                    wait_tile(dve, "out2", t, 0, layer)
                    nc.vector.tensor_tensor(h[:, t, :], h[:, t, :], bank_ap("out2", t), ALU.add)\
                        .then_inc(evacuated("out2", t), 1)
                    dve_add_square(dve, q + t, tmp2[:, sq_parity(7, t), :])
                ffn("up_b", "down_b", "xn_b", "ffn_b", n, norm_at(3, layer + 1)[1], layer)
            dve_norm(dve, N_LAST, D)
            for t in range(DT):
                scaled(dve, h[:, t, :], h[:, t, :], cols[:, COL1["final2"] + t:COL1["final2"] + t + 1], "result")


SQ_FIRST = {"down_a": 0, "down_b": 0}
SQ_OFF = {"down_a": (24 + 8) % 2, "down_b": (24 + 29) % 2}


def columns(v):
    return np.ascontiguousarray(v.reshape(-1, P).T)


def units(w, order, upc):
    K = w.shape[0] // P
    w = w[:, order].reshape(K, P, -1, P).transpose(2, 0, 1, 3).reshape(-1, upc, P, P)
    return np.ascontiguousarray(w.transpose(0, 2, 1, 3).reshape(-1, P, upc * P))


def wide(w):
    K = w.shape[0] // P
    return np.ascontiguousarray(w.reshape(K // 4, 4, P, S).transpose(0, 2, 1, 3).reshape(-1, P, 4 * S))


def lay_out(x):
    f = {k: np.asarray(v) for k, v in x.items()}
    A = {}
    A["x"] = np.ascontiguousarray(f["x"][0].T.reshape(DT, P, S).transpose(1, 0, 2))
    w_in = f["w_in"][0]
    every = np.arange(D)
    A["w_ada"] = units(f["w_ada"][0], np.arange(6 * D), 16)
    A["w_v"] = np.concatenate([wide(w_in[:, D + n * S:D + (n + 1) * S]) for n in range(2)])
    A["w_u"] = units(w_in, every, 16)
    A["w_qk"] = units(w_in, 2 * D + np.arange(2 * D), 16)
    A["w_mv"] = np.concatenate([wide(w_in[:, 4 * D + n * S:4 * D + (n + 1) * S]) for n in range(2)])
    A["w_o"] = units(w_in, 5 * D + every, 16)
    A["w_ga"] = units(w_in, 6 * D + 8 + every, 16)
    A["w_gb"] = units(w_in, 7 * D + 8 + every, 16)
    gates = np.zeros((DT, P, 36), np.float32)
    gates[:, :, 0:4] = w_in[:, 6 * D:6 * D + 4].reshape(DT, P, 4)
    gates[:, :, 32:36] = w_in[:, 6 * D + 4:6 * D + 8].reshape(DT, P, 4)
    A["w_if"] = np.ascontiguousarray(gates.transpose(1, 0, 2))
    A["gate_b"] = np.ascontiguousarray(f["mlstm_gate_b"][0].T)
    A["w_out1"] = units(f["w_out"][0], every, 16)
    A["w_ff1"] = units(f["w_ff1"][0], np.arange(4 * D), 16)
    A["w_ff2"] = units(f["w_ff2"][0], every, 16)
    A["ws_t"] = np.ascontiguousarray(f["gmlp_ws"][0].transpose(2, 0, 1))
    A["bs_row"] = np.ascontiguousarray(np.broadcast_to(f["gmlp_bs"][0][None], (P, GROUPS, P)))

    for n, tag in ((1, "a"), (2, "b")):
        ups, downs = [], []
        for layer in range(LAYERS):
            gate = f[f"ffn{n}_w_gate_2"][layer].reshape(D, F_TILES, 1, P)
            up = f[f"ffn{n}_w_up_2"][layer].reshape(D, F_TILES, 1, P)
            both = np.concatenate([gate, up], axis=2).reshape(D, -1)
            ups.append(units(both, np.arange(both.shape[1]), 16))
            downs.append(units(f[f"ffn{n}_w_down_2"][layer], every, F_TILES))
        A[f"w_up_{tag}"], A[f"w_down_{tag}"] = np.concatenate(ups), np.concatenate(downs)
    a0, b0, c0 = 0, 768, 1440
    kpe = np.tile(b0 + 640 + np.arange(ROPE), 4)
    order = np.concatenate([b0 + np.arange(384), b0 + 384 + np.arange(256), kpe, c0 + np.arange(512),
                            a0 + np.arange(512)])
    nope = (np.arange(B_HEADS)[:, None] * (NOPE + ROPE) + np.arange(NOPE)).ravel()
    roped = (np.arange(B_HEADS)[:, None] * (NOPE + ROPE) + NOPE + np.arange(ROPE)).ravel()
    k_cols = (np.arange(B_HEADS)[:, None] * 128 + np.arange(64)).ravel()
    w_in2, w_in_v, w_uq, w_ukv = [], [], [], []
    for layer in range(LAYERS):
        w = f["w_in_2"][layer]
        w_in2.append(units(w, order, 16))
        w_in_v.append(wide(np.concatenate([w[:, 512:768], w[:, 1952:2208]], axis=1)))
        w_uq.append(units(f["mla_w_uq_2"][layer], np.concatenate([nope, roped]), 9))
        ukv = f["mla_w_ukv_2"][layer]
        keys = units(ukv, k_cols, 8)
        vals = ukv[:, k_cols + 64].reshape(KV_TILES, P, S).transpose(1, 0, 2).reshape(1, P, 8 * P)
        w_ukv.append(np.concatenate([keys, vals], axis=2))
    A["w_in2"], A["w_in_v"] = np.concatenate(w_in2), np.concatenate(w_in_v)
    A["w_uq"], A["w_ukv"] = np.concatenate(w_uq), np.concatenate(w_ukv)
    A["w_out2"] = np.concatenate([units(f["w_out_2"][layer], every, 16) for layer in range(LAYERS)])

    half = ROPE // 2
    inv = (np.float32(10000.0) ** (-np.arange(half, dtype=np.float32) / np.float32(half))).astype(np.float32)
    sign = np.where(np.arange(ROPE) < half, -1.0, 1.0).astype(np.float32)
    parts = [columns(f["c"]), columns(f["b_ada"]), columns(f["norm1_g"])]
    parts += [columns(f["conv_w"][0, j]) for j in range(CONV_K)]
    parts += [columns(f[k]) for k in ("conv_b", "gmlp_ln_g", "gmlp_ln_b", "mlstm_hn_g", "norm2_g", "final_g",
                                      "final_norm_2")]
    parts += [np.tile(inv, P // half)[:, None], np.tile(sign, P // ROPE)[:, None]]
    for layer in range(LAYERS):
        parts += [columns(f[k][layer]) for k in ("ffn1_norm_2", "mix_norm_2", "mla_q_norm_2", "mla_kv_norm_2",
                                                 "ffn2_norm_2")]
        parts += [columns(np.tile(f["diff_head_norm_2"][layer], 2)), np.zeros((P, 1), np.float32)]
    A["cols"] = np.ascontiguousarray(np.concatenate(parts, axis=1))
    lam = np.stack([f[f"diff_lambda_{k}_2"] for k in ("q1", "k1", "q2", "k2")], axis=1)
    A["lam"] = np.ascontiguousarray(np.broadcast_to(lam[None], (P,) + lam.shape))
    pos = f["positions_2"].reshape(S).astype(np.int32)
    A["pos"] = np.ascontiguousarray(np.concatenate([np.broadcast_to(pos[None], (P, S)), pos.reshape(ST, P).T], axis=1))

    consts = np.zeros((P, N_CONSTS, P), np.float32)
    i = np.arange(P)
    consts[i, IDENT, i] = 1.0
    consts[i, SWAP, i ^ half] = 1.0
    consts[:, ONES, :] = 1.0
    consts[:, MEAN256, :] = 1.0 / HEAD_DIM
    consts[:, HEAD_ONES, :] = i[:, None] // 64 == i[None, :] // 64
    A["consts"] = consts
    off = np.abs(np.arange(S)[:, None] - np.arange(S)[None, :])
    count = sum(((off % d == 0) & (off // d <= w // 2 // d)).astype(int) for w, d in WINDOW_PATTERNS)
    logs = np.where(count > 0, np.log(np.maximum(count, 1)), -1e30) / SCALE_A
    A["log_c"] = np.ascontiguousarray(logs.astype(np.float32).reshape(ST, P, S).transpose(1, 0, 2))
    return A


def kernel(**inputs):
    import concourse.bacc as bacc
    from concourse.bass_utils import run_bass_kernel_spmd

    arrays = lay_out(inputs)
    nc = bacc.Bacc("TRN2", target_bir_lowering=False, num_devices=1)
    aps = {name: nc.dram_tensor(f"in_{name}", a.shape, mybir.dt.from_np(a.dtype), kind="ExternalInput").ap()
           for name, a in arrays.items()}
    out = nc.dram_tensor("out_t", (P, DT, S), F32, kind="ExternalOutput").ap()
    build(nc, aps, out)
    r = run_bass_kernel_spmd(nc, [{f"in_{name}": a for name, a in arrays.items()}], core_ids=[0])
    got = r.results[0]["out_t"]
    return np.ascontiguousarray(got.transpose(1, 0, 2).reshape(D, S).T)[None]
```
